# Optimizing a Trainium2 kernel written in Bass

```python
import math
import jax
import jax.numpy as jnp
from jax import lax
import numpy as np

'''Two layers of a chunk-causal hybrid streaming encoder (parallel head groups per layer).

Each layer: x += W_out[ GLA(group A) | short-gated-conv(group B) | diff-attention(group C) ](rmsnorm(x))
            x += FFN(rmsnorm(x))   (dense SwiGLU on even layers, top-2-of-8 SwiGLU experts on odd layers)
All three groups read one combined input projection of the same normalised input.

Inputs:
  x_prompt  (BATCH, SEQ, D_MODEL)            first SEQ frames of new streams, positions 0..SEQ-1
  x_sample  (DEC_BATCH, DEC_SEQ, D_MODEL)    next frames of running streams, positions PAST_LEN..
  state_gla (DEPTH, DEC_BATCH, H_A, DK_A, DV_A)        GLA recurrent matrix state
  state_conv(DEPTH, DEC_BATCH, CONV_W-1, W_B)          last 2 conv input rows (C*h)
  cache_k   (DEPTH, DEC_BATCH, PAST_LEN, H_C, 2, D_C)  diff-attn keys (k1,k2), QK-normed + rotary
  cache_v   (DEPTH, DEC_BATCH, PAST_LEN, H_C, DV_C)    diff-attn values
  followed by the weights.
Output tuple:
  (y_prompt (BATCH,SEQ,D_MODEL), y_sample (DEC_BATCH,DEC_SEQ,D_MODEL),
   k_prompt (DEPTH,BATCH,SEQ,H_C,2,D_C), v_prompt (DEPTH,BATCH,SEQ,H_C,DV_C),
   gla_prompt (DEPTH,BATCH,H_A,DK_A,DV_A), conv_prompt (DEPTH,BATCH,CONV_W-1,W_B),
   k_sample (DEPTH,DEC_BATCH,DEC_SEQ,H_C,2,D_C), v_sample (DEPTH,DEC_BATCH,DEC_SEQ,H_C,DV_C),
   gla_sample (DEPTH,DEC_BATCH,H_A,DK_A,DV_A), conv_sample (DEPTH,DEC_BATCH,CONV_W-1,W_B))
'''

D_MODEL = 1024
BATCH = 1
SEQ = 256
DEPTH = 2
DEC_BATCH = 1
DEC_SEQ = 64
PAST_LEN = 128

CHUNK = 64
Q_BLOCK = 128
EPS = 1e-6
ROPE_THETA = 10000.0

H_A = 4
DK_A = 48
DV_A = 96
GATE_RANK = 16
GATE_TAU = 16.0
W_B = 256
CONV_W = 3
H_C = 4
D_C = 48
DV_C = 2 * D_C

MIX_WIDTH = H_A * DV_A + W_B + H_C * DV_C
IN_SIZES = (H_A * DK_A, H_A * DK_A, H_A * DV_A, GATE_RANK, H_A * DV_A,
            W_B, W_B, W_B, H_C * 2 * D_C, H_C * 2 * D_C, H_C * DV_C)
N_IN = sum(IN_SIZES)

D_FF = 2816
N_EXPERTS = 8
TOP_K = 2
D_FF_E = 3584
N_DENSE = (DEPTH + 1) // 2
N_MOE = DEPTH // 2

kernel_name = 'hymba_gla_conv_diffattn_streaming_step'

F32 = jnp.float32

def rmsnorm(x, g):
    x32 = x.astype(F32)
    y = x32 * lax.rsqrt(jnp.mean(x32 * x32, axis=-1, keepdims=True) + EPS)
    return (y * g.astype(F32)).astype(x.dtype)

def rope(x, pos):
    half = x.shape[-1] // 2
    inv_freq = ROPE_THETA ** (-jnp.arange(half, dtype=F32) / half)
    ang = pos.astype(F32)[:, None] * inv_freq[None, :]
    cos = jnp.cos(ang)[None, :, None, None, :]
    sin = jnp.sin(ang)[None, :, None, None, :]
    x32 = x.astype(F32)
    x1, x2 = x32[..., :half], x32[..., half:]
    return jnp.concatenate([x1 * cos - x2 * sin, x2 * cos + x1 * sin], axis=-1).astype(x.dtype)

def split_cols(proj):
    outs, off = [], 0
    for n in IN_SIZES:
        outs.append(proj[..., off:off + n])
        off += n
    return outs

def gla_chunk(s0, q, k, v, lg):
    q32, k32, v32 = q.astype(F32), k.astype(F32), v.astype(F32)
    b = jnp.cumsum(lg.astype(F32), axis=1)
    L = q.shape[1]
    causal = jnp.tril(jnp.ones((L, L), dtype=bool))
    diff = b[:, :, None] - b[:, None, :]
    decay = jnp.exp(jnp.where(causal[None, :, :, None, None], diff, -jnp.inf))
    att = jnp.einsum('bthd,bshd,btshd->bhts', q32, k32, decay)
    o = jnp.einsum('bhts,bshe->bthe', att, v32) + jnp.einsum('bthd,bhde->bthe', q32 * jnp.exp(b), s0)
    b_last = b[:, -1]
    k_dec = k32 * jnp.exp(b_last[:, None] - b)
    s1 = jnp.exp(b_last)[..., None] * s0 + jnp.einsum('bshd,bshe->bhde', k_dec, v32)
    return s1, o

def gla_recurrence(s0, q, k, v, lg):
    B, L = q.shape[:2]
    if L <= CHUNK:
        s1, o = gla_chunk(s0, q, k, v, lg)
        return o, s1
    n = L // CHUNK

    def to_chunks(a):
        return jnp.moveaxis(a.reshape((B, n, CHUNK) + a.shape[2:]), 1, 0)

    def step(s, xs):
        return gla_chunk(s, *xs)

    s_last, o = lax.scan(step, s0, (to_chunks(q), to_chunks(k), to_chunks(v), to_chunks(lg)))
    o = jnp.moveaxis(o, 0, 1).reshape(B, L, H_A, DV_A)
    return o, s_last

def short_conv(bg, cg, hg, w_conv, buf):
    u = cg * hg
    up = jnp.concatenate([buf, u], axis=1)
    L = u.shape[1]
    y = w_conv[0] * up[:, 0:L]
    for j in range(1, CONV_W):
        y = y + w_conv[j] * up[:, j:j + L]
    return bg * y, up[:, -(CONV_W - 1):]

def diff_core(q, k, v, lam, mask):
    s = jnp.einsum('bqhcd,bkhcd->bhcqk', q, k, preferred_element_type=F32) * (D_C ** -0.5)
    if mask is not None:
        s = jnp.where(mask, s, -jnp.inf)
    p = jax.nn.softmax(s, axis=-1)
    a = p[:, :, 0] - lam * p[:, :, 1]
    return jnp.einsum('bhqk,bkhe->bqhe', a, v.astype(F32))

def diff_prompt(q, k, v, lam):
    B, S = q.shape[:2]
    nb = S // Q_BLOCK
    qb = jnp.swapaxes(q.reshape(B, nb, Q_BLOCK, H_C, 2, D_C), 0, 1)
    k_chunk = jnp.arange(S) // CHUNK

    def block(args):
        qi, i = args
        q_chunk = (i * Q_BLOCK + jnp.arange(Q_BLOCK)) // CHUNK
        mask = k_chunk[None, :] <= q_chunk[:, None]
        return diff_core(qi, k, v, lam, mask)

    o = lax.map(block, (qb, jnp.arange(nb)))
    return jnp.swapaxes(o, 0, 1).reshape(B, S, H_C, DV_C)

def swiglu(x, wg, wu, wd):
    return (jax.nn.silu(x @ wg) * (x @ wu)) @ wd

def moe_ffn(x, w_r, wg, wu, wd):
    B, L, D = x.shape
    xt = x.reshape(-1, D)
    logits = jnp.dot(xt, w_r, preferred_element_type=F32)
    top_v, top_i = lax.top_k(logits, TOP_K)
    w = jax.nn.softmax(top_v, axis=-1)
    gates = jnp.einsum('tk,tke->te', w, jax.nn.one_hot(top_i, N_EXPERTS, dtype=F32))
    y = jnp.zeros(xt.shape, F32)
    for e in range(N_EXPERTS):
        h = jax.nn.silu(xt @ wg[e]) * (xt @ wu[e])
        y = y + gates[:, e:e + 1] * jnp.dot(h, wd[e], preferred_element_type=F32)
    return y.astype(x.dtype).reshape(B, L, D)

def hybrid_layer(x, pos, gla_s0, conv_buf, k_past, v_past, lam_init,
                 g_mix, w_in, w_g2, b_g2, g_gla, w_conv, g_q, g_k,
                 lq1, lk1, lq2, lk2, g_sub, w_out, g_ffn, ffn):
    Bsz, L, _ = x.shape
    dt = x.dtype
    xn = rmsnorm(x, g_mix)
    qa, ka, va, ga, ra, bb, cb, hb, qc, kc, vc = split_cols(xn @ w_in)
    q = qa.reshape(Bsz, L, H_A, DK_A) * (DK_A ** -0.5)
    k = ka.reshape(Bsz, L, H_A, DK_A)
    v = va.reshape(Bsz, L, H_A, DV_A)
    lg = (jax.nn.log_sigmoid((ga @ w_g2 + b_g2).astype(F32)) / GATE_TAU).reshape(Bsz, L, H_A, DK_A)
    s0 = jnp.zeros((Bsz, H_A, DK_A, DV_A), F32) if gla_s0 is None else gla_s0.astype(F32)
    o_a, s1 = gla_recurrence(s0, q, k, v, lg)
    y_a = rmsnorm(o_a.astype(dt), g_gla).reshape(Bsz, L, H_A * DV_A) * jax.nn.silu(ra)
    buf0 = jnp.zeros((Bsz, CONV_W - 1, W_B), dt) if conv_buf is None else conv_buf
    y_b, buf1 = short_conv(bb, cb, hb, w_conv, buf0)
    lam = (jnp.exp(jnp.sum(lq1.astype(F32) * lk1.astype(F32)))
           - jnp.exp(jnp.sum(lq2.astype(F32) * lk2.astype(F32))) + lam_init)
    qd = rope(rmsnorm(qc.reshape(Bsz, L, H_C, 2, D_C), g_q), pos)
    kd = rope(rmsnorm(kc.reshape(Bsz, L, H_C, 2, D_C), g_k), pos)
    vd = vc.reshape(Bsz, L, H_C, DV_C)
    if k_past is None:
        o_c = diff_prompt(qd, kd, vd, lam)
    else:
        o_c = diff_core(qd, jnp.concatenate([k_past, kd], axis=1),
                        jnp.concatenate([v_past, vd], axis=1), lam, None)
    y_c = (rmsnorm(o_c.astype(dt), g_sub) * (1.0 - lam_init)).reshape(Bsz, L, H_C * DV_C)
    x = x + jnp.concatenate([y_a, y_b, y_c], axis=-1) @ w_out
    x = x + ffn(rmsnorm(x, g_ffn))
    return x, kd, vd, s1.astype(dt), buf1

def setup_inputs(seed: int = 0) -> dict:
    key = jax.random.key(seed)
    it = iter(list(jax.random.split(key, 32)))

    def nrm(shape, scale):
        return jax.random.normal(next(it), shape, F32) * scale

    def gain(shape):
        return 1.0 + 0.02 * jax.random.normal(next(it), shape, F32)

    return {
        'x_prompt': nrm((BATCH, SEQ, D_MODEL), 1.0),
        'x_sample': nrm((DEC_BATCH, DEC_SEQ, D_MODEL), 1.0),
        'state_gla': nrm((DEPTH, DEC_BATCH, H_A, DK_A, DV_A), 0.5),
        'state_conv': nrm((DEPTH, DEC_BATCH, CONV_W - 1, W_B), 1.0),
        'cache_k': nrm((DEPTH, DEC_BATCH, PAST_LEN, H_C, 2, D_C), 1.0),
        'cache_v': nrm((DEPTH, DEC_BATCH, PAST_LEN, H_C, DV_C), 1.0),
        'g_mix': gain((DEPTH, D_MODEL)),
        'w_in': nrm((DEPTH, D_MODEL, N_IN), D_MODEL ** -0.5),
        'w_g2': nrm((DEPTH, GATE_RANK, H_A * DK_A), GATE_RANK ** -0.5),
        'b_g2': nrm((DEPTH, H_A * DK_A), 0.1),
        'g_gla': gain((DEPTH, DV_A)),
        'w_conv': nrm((DEPTH, CONV_W, W_B), CONV_W ** -0.5),
        'g_q': gain((DEPTH, D_C)),
        'g_k': gain((DEPTH, D_C)),
        'lambda_q1': nrm((DEPTH, D_C), 0.1),
        'lambda_k1': nrm((DEPTH, D_C), 0.1),
        'lambda_q2': nrm((DEPTH, D_C), 0.1),
        'lambda_k2': nrm((DEPTH, D_C), 0.1),
        'g_sub': gain((DEPTH, DV_C)),
        'w_out': nrm((DEPTH, MIX_WIDTH, D_MODEL), MIX_WIDTH ** -0.5),
        'g_ffn': gain((DEPTH, D_MODEL)),
        'ffn_w_gate': nrm((N_DENSE, D_MODEL, D_FF), D_MODEL ** -0.5),
        'ffn_w_up': nrm((N_DENSE, D_MODEL, D_FF), D_MODEL ** -0.5),
        'ffn_w_down': nrm((N_DENSE, D_FF, D_MODEL), D_FF ** -0.5),
        'w_router': nrm((N_MOE, D_MODEL, N_EXPERTS), D_MODEL ** -0.5),
        'moe_w_gate': nrm((N_MOE, N_EXPERTS, D_MODEL, D_FF_E), D_MODEL ** -0.5),
        'moe_w_up': nrm((N_MOE, N_EXPERTS, D_MODEL, D_FF_E), D_MODEL ** -0.5),
        'moe_w_down': nrm((N_MOE, N_EXPERTS, D_FF_E, D_MODEL), D_FF_E ** -0.5),
    }

def reference(x_prompt, x_sample, state_gla, state_conv, cache_k, cache_v,
              g_mix, w_in, w_g2, b_g2, g_gla, w_conv, g_q, g_k,
              lambda_q1, lambda_k1, lambda_q2, lambda_k2, g_sub, w_out, g_ffn,
              ffn_w_gate, ffn_w_up, ffn_w_down, w_router, moe_w_gate, moe_w_up, moe_w_down):
    pos_p = jnp.arange(x_prompt.shape[1])
    pos_s = cache_k.shape[2] + jnp.arange(x_sample.shape[1])
    hp, hs = x_prompt, x_sample
    kp, vp, sp, cp = [], [], [], []
    ks, vs, ss, cs = [], [], [], []
    for l in range(DEPTH):
        lam_init = 0.8 - 0.6 * math.exp(-0.3 * l)
        i = l // 2
        if l % 2 == 0:
            def ffn(z, i=i):
                return swiglu(z, ffn_w_gate[i], ffn_w_up[i], ffn_w_down[i])
        else:
            def ffn(z, i=i):
                return moe_ffn(z, w_router[i], moe_w_gate[i], moe_w_up[i], moe_w_down[i])
        shared = (g_mix[l], w_in[l], w_g2[l], b_g2[l], g_gla[l], w_conv[l], g_q[l], g_k[l],
                  lambda_q1[l], lambda_k1[l], lambda_q2[l], lambda_k2[l], g_sub[l], w_out[l], g_ffn[l], ffn)
        hp, k_, v_, s_, c_ = hybrid_layer(hp, pos_p, None, None, None, None, lam_init, *shared)
        kp.append(k_); vp.append(v_); sp.append(s_); cp.append(c_)
        hs, k_, v_, s_, c_ = hybrid_layer(hs, pos_s, state_gla[l], state_conv[l],
                                          cache_k[l], cache_v[l], lam_init, *shared)
        ks.append(k_); vs.append(v_); ss.append(s_); cs.append(c_)
    return (hp, hs, jnp.stack(kp), jnp.stack(vp), jnp.stack(sp), jnp.stack(cp),
            jnp.stack(ks), jnp.stack(vs), jnp.stack(ss), jnp.stack(cs))


_drawn_inputs = setup_inputs


def setup_inputs(seed=0):
    import zlib

    import numpy as np

    out = dict(_drawn_inputs(seed))
    spreads = {}
    factors = {'g_gla': 8.863, 'g_sub': 4.133, 'g_ffn': 3.105}
    for name, (base, spread) in spreads.items():
        noise = np.random.default_rng([zlib.crc32(name.encode()), seed]).standard_normal(out[name].shape)
        drawn = base * np.exp(spread * noise) if base else spread * noise
        out[name] = jnp.asarray(drawn.astype(out[name].dtype))
    for name, factor in factors.items():
        out[name] = (out[name] * factor).astype(out[name].dtype)
    return out
```

```python
from contextlib import ExitStack

import numpy as np
import concourse.bass as bass
from concourse import mybir

F32 = mybir.dt.float32
FR = mybir.dt.float32r
I32 = mybir.dt.int32
U32 = mybir.dt.uint32
ALU = mybir.AluOpType
ACT = mybir.ActivationFunctionType
AX_X = mybir.AxisListType.X

P = 128
D = 1024
KB = D // P
SEQ, DEC, PAST = 256, 64, 128
T = SEQ + DEC
TILES = [(0, 128), (128, 128), (256, 64)]
NT = len(TILES)
CH = 64
CHUNKS = [(0, 0), (0, 64), (1, 0), (1, 64), (2, 0)]
H = 4
DK = 48
DV = 96
HW = 64
GR = 16
DEPTH = 2
EPS = 1e-6
FF = 2816
FB = FF // P
NE = 8
FE = 3584
FC = FE // 512
FEB = FE // P
MAXB = 3
LAM0 = [0.8 - 0.6 * float(np.exp(-0.3 * l)) for l in range(DEPTH)]
SC = DK ** -0.5

QA, KA, VA, GA, RA = 0, 192, 384, 768, 784
BB, CB, HB = 1168, 1424, 1680
QC, KC, VC = 1936, 2320, 2704

CONST = {}
_at = 0
for _name, _w in [("ident", 128), ("tri", 128), ("ones", 128), ("scan", T), ("cc", NT * DK), ("ss", NT * DK),
                  ("tok", NT), ("iota8", 8), ("slot", MAXB * P), ("attm", H * CH), ("rowsel", P), ("neg", CH)]:
    CONST[_name] = (_at, _w)
    _at += _w
CONST_W = _at

RING = 4
SLOT = KB * 512

UNITS = []
for _l in range(DEPTH):
    UNITS += [("qk", _l), ("bc", _l), ("hb", _l), ("kc", _l), ("qc", _l), ("vc", _l), ("va", _l), ("ra", _l),
              ("wo", _l, 0), ("wo", _l, 1)]
    if _l == 0:
        for _j in range((FB + 3) // 4):
            UNITS += [("g", _j), ("u", _j)]
        UNITS += [("d", _j) for _j in range((FB + 3) // 4)]
UNIT = {u: n for n, u in enumerate(UNITS)}
U0 = len(UNITS)
UE = 3 * FC
PIECE = SLOT // 2
NP = 2 * UE
PR = 7
SR = 3
assert 2 * NP % PR == 0 and 2 * NP % SR == 0 and PR * PIECE <= RING * SLOT


HT_AT = [4 * _j + 11 for _j in range(FC - 1)] + [4 * FC + 7]
X_AT = NP - 3

JOBS_A, JOBS_D, JOBS_S = [], [], []


def _norm_jobs(i):
    for t in range(NT):
        JOBS_A.append(("xt", i, t))
        JOBS_D.append(("xt", i, t))


JOBS_A += [("par",), ("bcast", 0)]
JOBS_D += [("bcast", 1)]
for _l in range(DEPTH):
    _norm_jobs(2 * _l)
    JOBS_A += [("ga", _l)] + [("qk", _l, t) for t in range(NT)] + [("qkt", _l, t) for t in range(NT)]
    JOBS_A += [("bb", _l, 0), ("bb", _l, 1), ("cb", _l, 0), ("cb", _l, 1)]
    JOBS_D += [("gl", _l, 0), ("gl", _l, 1), ("hb", _l, 0), ("hb", _l, 1)]
    JOBS_D += [("kc", _l, t) for t in range(NT)] + [("qc", _l, t) for t in range(NT)]
    JOBS_A += [("pk", _l)] + [("kt", _l, t) for t in range(NT)] + [("vc", _l, t) for t in range(NT)]
    JOBS_A += [("qt", _l, t) for t in range(NT)] + [("va", _l, t) for t in range(NT)]
    JOBS_D += [("ra", _l, t) for t in range(NT)]
    JOBS_A += [("kd", _l, t) for t in range(NT)]
    JOBS_D += [("att", _l, t) for t in range(NT)] + [("U", _l, c) for c in range(len(CHUNKS))]
    JOBS_D += [("oa", _l, t) for t in range(NT)]
    JOBS_S += [("s", _l, n) for n in range(NT * H)]
    JOBS_A += [("at", _l, n) for n in range(NT * H)]
    JOBS_D += [("oc", _l, t) for t in range(NT)]
    JOBS_A += [("ya", _l, t) for t in range(NT)] + [("yc", _l, t) for t in range(NT)]
    for t in range(NT):
        JOBS_A.append(("wo", _l, t))
        JOBS_D.append(("wo", _l, t))
    _norm_jobs(2 * _l + 1)
    if _l == 0:
        for _f in range(FB):
            JOBS_A.append(("g", _f))
            JOBS_D.append(("u", _f))
        for t in range(NT):
            JOBS_A.append(("dn", t))
            JOBS_D.append(("dn", t))
JOBS_D += [("lg", t) for t in range(NT)] + [("rk", t) for t in range(NT)] + [("cnt",), ("idx",)]


class PsumRing:

    def __init__(self, banks, jobs, full, free):
        self.banks, self.full, self.free = banks, full, free
        self.n = {j: i for i, j in enumerate(jobs)}
        self.count = len(jobs)

    def bank(self, job):
        return self.banks[self.n[job] % len(self.banks)]

    def begin(self, pe, job):
        n = self.n[job]
        if n >= len(self.banks):
            pe.wait_ge(self.free, n - len(self.banks) + 1)
        return self.bank(job)

    def filled(self, job):
        return self.n[job] + 1

    emptied = filled


class Steps:

    def __init__(self, eng, sem):
        self.eng, self.sem, self.n = eng, sem, 0

    def __call__(self, ins):
        ins.then_inc(self.sem, 1)
        self.n += 1
        self.eng.wait_ge(self.sem, self.n)


def build(nc, A, O):
    (y_p, y_s, k_p, v_p, gla_p, conv_p, k_s, v_s, gla_s, conv_s) = O
    hx = nc.dram_tensor("normed_rows", (T, D), F32, kind="Internal").ap()
    ybuf = nc.dram_tensor("expert_rows", (MAXB * NE * P, D), F32, kind="Internal").ap()

    with ExitStack() as ctx:
        def sb(name, shape, dt=F32, stack=ctx):
            return stack.enter_context(nc.sbuf_tensor(name, shape, dt))

        def sem(name):
            return ctx.enter_context(nc.semaphore(name))

        banks = [ctx.enter_context(nc.psum_tensor(f"bank{i}", [P, 512], F32)) for i in range(8)]
        A_full, A_free = sem("A_full"), sem("A_free")
        D_full, D_free = sem("D_full"), sem("D_free")
        S_full, S_free = sem("S_full"), sem("S_free")
        RA_ = PsumRing(banks[0:3], JOBS_A, A_full, A_free)
        RD_ = PsumRing(banks[3:6], JOBS_D, D_full, D_free)
        RS_ = PsumRing(banks[6:8], JOBS_S, S_full, S_free)

        x = sb("x", [P, NT, D])
        ring = sb("ring", [P, RING, SLOT])
        const = sb("const_sb", [P, CONST_W])
        pcol = sb("pcol", [P, 48])
        bc = sb("bc", [P, 960])
        wga = sb("wga", [P, DEPTH, KB, GR])
        wg2 = sb("wg2", [GR, DEPTH, 2, P])
        wr = sb("wr", [P, KB, NE])
        small_ss = sb("small_ss", [P, 18 * DEPTH, 8])
        small_rs = sb("small_rs", [P, 18 * DEPTH, 8])
        half_neg = sb("half_neg", [P, 8])
        zeros = sb("zeros", [P, D])
        CG = sb("CG", [P, DEPTH, 2, NT, DK])
        SG = sb("SG", [P, DEPTH, 2, NT, DK])
        lamt = sb("lamt", [P, 2, DEPTH])
        neglam = sb("neglam", [P, DEPTH])

        def C(name, rows=P):
            a, w = CONST[name]
            return const[0:rows, a:a + w]

        ident = C("ident")
        cc = C("cc").rearrange("p (t d) -> p t d", t=NT)
        ssn = C("ss").rearrange("p (t d) -> p t d", t=NT)

        def gcol(norm):
            at = (norm % 2) * 16 + (norm // 2) * 8
            return pcol[:, at:at + 8]

        def wconv(l, j, b):
            at = 32 + l * 6 + j * 2 + b
            return pcol[:, at:at + 1]

        def bg2(l, pair):
            return pcol[:, 44 + 2 * l + pair:45 + 2 * l + pair]

        bq = bc[:, 0:192].rearrange("p (w l d) -> p w l d", w=2, l=DEPTH)
        bl = bc[:, 192:576].rearrange("p (v l d) -> p v l d", v=4, l=DEPTH)
        bgla = bc[:, 576:768].rearrange("p (l d) -> p l d", l=DEPTH)
        bsub = bc[:, 768:960].rearrange("p (l d) -> p l d", l=DEPTH)

        front = ExitStack()
        xhat = sb("xhat", [P, NT, D], F32, front)
        xT = sb("xT", [P, KB, T], F32, front)
        mix = ExitStack()

        def mb(name, shape, dt=F32):
            return sb(name, shape, dt, mix)

        over = sb("over", [P, 8192], F32, front)
        taken = [0]

        def ov_(*shape):
            n = int(np.prod(shape))
            a = over[:, taken[0]:taken[0] + n]
            taken[0] += n
            assert taken[0] <= 8192
            names = " ".join("abc"[:len(shape)])
            return a.rearrange(f"p ({names}) -> p {names}", **dict(zip("abc", shape)))

        qT, kT = ov_(H, T), ov_(H, T)
        va, vc, sra = ov_(NT, H * DV), ov_(NT, H * DV), ov_(NT, H * DV)
        up, bbs, cbs = ov_(2, T + 4), ov_(2, T), ov_(2, T)
        Yc = sra
        yb = cbs
        gla = mb("gla", [P, 9, 2, T])
        qr, kr, cum, d1, z, e1, ed, eb, qb = [gla[:, i] for i in range(9)]
        eq, ek = z, e1
        glaf = gla[:].rearrange("p i r n -> p (i r n)")
        yv = glaf[:, 2 * 2 * T:2 * 2 * T + 2 * (T + 2)].rearrange("p (b n) -> p b n", b=2)
        pe_ = glaf[:, 0:1024].rearrange("p (i c k) -> p i c k", i=2, c=2)
        am = glaf[:, 1024:1536].rearrange("p (i k) -> p i k", i=2)
        aT = glaf[:, 1536:2048].rearrange("p (i b n) -> p i b n", i=2, b=2)
        atm = glaf[:, 2048:2304]
        kdn = mb("kdn", [P, NT, 2, P])
        Ya = mb("Ya", [P, NT, H * DV])
        Yaf = Ya[:].rearrange("p t n -> p (t n)")
        brow, prow = Yaf[0:1, 0:960], Yaf[0:48, 960:960 + P]
        sq = mb("sq", [P, 2, H * DV])
        t1 = mb("t1", [P, 8 * DK])
        t2 = mb("t2", [P, 8 * DK])
        t3 = mb("t3", [P, 8 * DK])
        gaT = t2[0:GR, 0:T]
        pkr = mb("pkr", [P, 8, HW])
        pkT = mb("pkT", [P, H, PAST])
        pv = mb("pv", [P, DEPTH, H * DV])
        att = mb("att", [P, NT, H, CH])
        mx = mb("mx", [P, 2, 2])
        nm = mb("nm", [P, 2, 2])
        sm = mb("sm", [P, 2, 2])
        rc = mb("rc", [P, 2])
        rc2 = mb("rc2", [P, 1])
        S = mb("S", [P, len(CHUNKS) + 1, 2, DV])
        krope = xhat[:, :, 0:512].rearrange("p t (g c) -> p t g c", c=HW)
        qrope = xhat[:, :, 512:1024].rearrange("p t (g c) -> p t g c", c=HW)
        qkp = qrope
        yT = xT
        mix.close()

        ffn = ExitStack()
        hT = sb("hT", [P, FB, T], F32, ffn)
        sg = sb("sg", [P, 2, T], F32, ffn)
        ffn.close()

        front.close()
        hmT_hi = sb("hmT_hi", [P, FEB, P], FR)
        ye = sb("ye", [P, D])
        hm = sb("hm", [P, 2, 512])
        split_hi = sb("split_hi", [P, SR, PIECE], FR)
        split_lo = sb("split_lo", [P, SR, PIECE], FR)
        lgs = sb("lgs", [P, NT, NE])
        top = sb("top", [P, NT, 8])
        topi = sb("topi", [P, NT, 8], U32)
        topf = sb("topf", [P, NT, 8])
        oh = sb("oh", [P, NT, 2, NE])
        M = sb("M", [P, NT, NE])
        rank = sb("rank", [P, NT, NE])
        rtmp = sb("rtmp", [P, 2, NE])
        rk2 = sb("rk2", [P, NT, 2])
        ov = sb("ov", [P, 2])
        posf = sb("posf", [P, NT, 2])
        pos = sb("pos", [P, NT, 2], U32)
        gd = sb("gd", [P, NT, 4])
        cntm = sb("cntm", [P, 4])
        npair = sb("npair", [1, 2], I32)
        rankm = sb("rankm", [P, NT, NE])
        idx = sb("idx", [P, MAXB * NE + 1], U32)
        idc = sb("idc", [P, 1], U32)
        xg = sb("xg", [P, D])
        xgT_hi = sb("xgT_hi", [P, KB, P], FR)
        xgT_lo = sb("xgT_lo", [P, KB, P], FR)
        hs = sb("hs", [P, 2, 512])
        routing = ExitStack()
        G = sb("G", [P, 2, NT, MAXB * P], F32, routing)
        routing.close()
        loop_only = ExitStack()
        hmT_lo = sb("hmT_lo", [P, FEB, P], FR, loop_only)
        loop_only.close()
        cmb = sb("cmb", [P, 2, D])

        const_in, prow_in, brow_in, x_in, w_small = sem("const_in"), sem("prow_in"), sem("brow_in"), sem("x_in"), sem("w_small")
        prow_zero, wg2_zero, pool_zero = sem("prow_zero"), sem("wg2_zero"), sem("pool_zero")
        past_in, hist_in, s0_in = sem("past_in"), sem("hist_in"), sem("s0_in")
        ring_full = [sem(f"ring_full{i}") for i in range(RING)]
        piece_full = [sem(f"piece_full{i}") for i in range(PR)]
        hi_ready, lo_ready, piece_used, th_ready = sem("hi_ready"), sem("lo_ready"), sem("piece_used"), sem("th_ready")
        unit_used = sem("unit_used")
        bcast_ready, tables_ready, lam_exp = sem("bcast_ready"), sem("tables_ready"), sem("lam_exp")
        rows_sq, ss_ready, rs_ready = sem("rows_sq"), sem("ss_ready"), sem("rs_ready")
        xhat_ready = sem("xhat_ready")
        sq_ready = sem("sq_ready")
        ln_ready, d_ready, exps_ready, gk_ready = sem("ln_ready"), sem("d_ready"), sem("exps_ready"), sem("gk_ready")
        rope_ready, att_ready, state_ready, conv_ready = sem("rope_ready"), sem("att_ready"), sem("state_ready"), sem("conv_ready")
        era_ready, ya_ready, yc_ready = sem("era_ready"), sem("ya_ready"), sem("yc_ready")
        nm_ready, am_ready = sem("nm_ready"), sem("am_ready")
        k_out, v_out, st_out, cv_out, y_out = sem("k_out"), sem("v_out"), sem("st_out"), sem("cv_out"), sem("y_out")
        hx_out, gate_in, gate_out, M_ready = sem("hx_out"), sem("gate_in"), sem("gate_out"), sem("M_ready")
        G_ready, G_used, idx_ready, pairs_ready, pos_ready = sem("G_ready"), sem("G_used"), sem("idx_ready"), sem("pairs_ready"), sem("pos_ready")
        idc_ready, xg_in, ye_out, rows_out = sem("idc_ready"), sem("xg_in"), sem("ye_out"), sem("rows_out")
        g_free, u_free = sem("g_free"), sem("u_free")
        t_full, t_free, y_free = sem("t_full"), sem("t_free"), sem("y_free")
        cmb_in, cmb_used = [sem(f"cmb_in{k}") for k in range(2)], sem("cmb_used")
        pe_step, dve_step, act_step, pool_step = sem("pe_step"), sem("dve_step"), sem("act_step"), sem("pool_step")

        raw = ring[:].rearrange("p s n -> p (s n)")

        NS = 12

        def rs_slot(l, what, t):
            return 18 * l + {"mix": 0, "kc": 3, "qc": 6, "oa": 9, "oc": 12, "ffn": 15}[what] + t

        def ss_count(l, what, t):
            return NS * l + {"kc": 0, "qc": 3, "oa": 6, "oc": 9}[what] + t + 1

        block = ctx.enter_context(nc.Block())

        def outputs_left(eng, l):
            eng.wait_ge(v_out, 16 * 2 * (l + 1))
            eng.wait_ge(st_out, 16 * 4 * (l + 1))
            eng.wait_ge(cv_out, 16 * 4 * (l + 1))

        @block.sync
        def _(sp):
            def cols(w, a, n):
                return w[:, a:a + n].rearrange("(k p) n -> p k n", p=P)

            def source(u):
                kind = u[0]
                if kind in ("g", "u"):
                    w = A["ffn_w_gate" if kind == "g" else "ffn_w_up"]
                    n = min(512, FF - 512 * u[1])
                    return cols(w[0], 512 * u[1], n), (KB, n)
                if kind == "d":
                    n = min(4, FB - 4 * u[1])
                    return A["ffn_w_down"][0, 512 * u[1]:512 * u[1] + P * n, :].rearrange("(b p) n -> p b n", p=P), (n, D)
                if kind == "wo":
                    return A["w_out"][u[1], 512 * u[2]:512 * u[2] + 512, :].rearrange("(b p) n -> p b n", p=P), (4, D)
                a, n = {"qk": (QA, 384), "bc": (BB, 512), "hb": (HB, 256), "kc": (KC, 384), "qc": (QC, 384),
                        "vc": (VC, 384), "va": (VA, 384), "ra": (RA, 384)}[kind]
                return cols(A["w_in"][u[1]], a, n), (KB, n)

            for n, u in enumerate(UNITS):
                src, (b, w) = source(u)
                if n >= RING:
                    sp.wait_ge(unit_used, n - RING + 1)
                sp.dma_start(ring[:, n % RING, 0:b * w].rearrange("p (b n) -> p b n", b=b), src).then_inc(ring_full[n % RING], 16)

            wg_v = A["moe_w_gate"][0].rearrange("e (k p) n -> e p k n", p=P)
            wu_v = A["moe_w_up"][0].rearrange("e (k p) n -> e p k n", p=P)
            wd_v = A["moe_w_down"][0].rearrange("e (c b p) n -> e c p b n", b=4, p=P)

            def pair(e, first):
                for i in range(2 * NP):
                    h, q = divmod(i, NP)
                    j, half = q // 2, q % 2
                    s = i % PR
                    sp.wait_ge(lo_ready, first + (i + 1))
                    if j < 2 * FC:
                        w = wg_v if j % 2 == 0 else wu_v
                        src = w[bass.ds(e + h, 1), :, 4 * half:4 * half + 4, 512 * (j // 2):512 * (j // 2) + 512]
                    else:
                        src = wd_v[bass.ds(e + h, 1), j - 2 * FC, :, 2 * half:2 * half + 2, :]
                    src = src.rearrange("e p k n -> p (e k) n")
                    dst = raw[:, s * PIECE:(s + 1) * PIECE].rearrange("p (k n) -> p k n", k=src.shape[1])
                    sp.dma_start(dst, src).then_inc(piece_full[s], 16)

            sp.wait_ge(unit_used, U0)
            sp.wait_ge(lo_ready, PR)
            with sp.Fori(0, NE // 2) as ip:
                pair(ip * 2, ip * (2 * NP))
            sp.wait_ge(pairs_ready, 1)
            more = sp.value_load(npair[0:1, 1:2], min_val=0, max_val=NE // 2 * (MAXB - 1))
            with sp.If(more > 0):
                with sp.Fori(0, more) as ip:
                    pair((ip % (NE // 2)) * 2, ip * (2 * NP) + NE * NP)

        @block.gpsimd
        def _(pool):
            step = Steps(pool, pool_step)
            nc.gpsimd.memset(prow, 0.0).then_inc(prow_zero, 1)
            pool.wait_ge(prow_zero, 1)
            pool.dma_start(prow[0:16, :], A["g_mix"].rearrange("l (k p) -> (l k) p", p=P)).then_inc(prow_in, 16)
            pool.dma_start(prow[16:32, :], A["g_ffn"].rearrange("l (k p) -> (l k) p", p=P)).then_inc(prow_in, 16)
            pool.dma_start(prow[32:44, :], A["w_conv"].rearrange("l j (b p) -> (l j b) p", p=P)).then_inc(prow_in, 16)
            pool.dma_start(prow[44:48, :].rearrange("r (h d) -> r h d", d=HW)[:, :, 0:DK],
                           A["b_g2"].rearrange("l (r h d) -> (l r) h d", r=2, h=2)).then_inc(prow_in, 16)
            step(nc.gpsimd.memset(wg2[:], 0.0))
            for l in range(DEPTH):
                for r in range(2):
                    pool.dma_start(wg2[:, l, r, :].rearrange("g (h d) -> g h d", d=HW)[:, :, 0:DK],
                                   A["w_g2"][l].rearrange("g (r h d) -> g r h d", r=2, h=2)[:, r]).then_inc(w_small, 16)
                pool.dma_start(wga[:, l], A["w_in"][l, :, GA:GA + GR].rearrange("(k p) n -> p k n", p=P),
                               ).then_inc(w_small, 16)
            pool.dma_start(wr[:], A["w_router"][0].rearrange("(k p) n -> p k n", p=P)).then_inc(w_small, 16)
            for tile in (att[:], S[:], up, pkr[:], zeros[:]):
                nc.gpsimd.memset(tile, 0.0).then_inc(pool_zero, 1)
            nc.gpsimd.memset(half_neg[:], -0.5).then_inc(pool_zero, 1)
            pool.wait_ge(pool_zero, 6)

            def loads(l):
                pool.dma_start(pkr[:, :, 0:DK], A["cache_k"][l, 0].rearrange("t h c d -> t (h c) d")).then_inc(past_in, 16)
                pool.dma_start(pv[:, l, :], A["cache_v"][l, 0].rearrange("t h d -> t (h d)")).then_inc(past_in, 16)
                for h in range(2):
                    pool.dma_start(S[HW * h:HW * h + DK, 5], A["state_gla"][l, 0].rearrange("(r h) d e -> h d r e", h=2)[h]).then_inc(s0_in, 16)
                for b in range(2):
                    with nc.allow_non_contiguous_dma(reason="two columns of history"):
                        pool.dma_start(up[:, b, SEQ + 2:SEQ + 4], A["state_conv"][l, 0, :, b * P:b * P + P].rearrange("j p -> p j")).then_inc(hist_in, 16)

            loads(0)

            pool.wait_ge(const_in, 16)
            pool.wait_ge(bcast_ready, 1)
            hd = DK // 2
            for l in range(DEPTH):
                for w in range(2):
                    g = bq[:, w, l, :]
                    nc.gpsimd.tensor_tensor(CG[:, l, w], cc, g.unsqueeze(1).to_broadcast([P, NT, DK]), ALU.mult)
                    nc.gpsimd.tensor_tensor(SG[:, l, w, :, 0:hd], ssn[:, :, 0:hd], g[:, hd:DK].unsqueeze(1).to_broadcast([P, NT, hd]), ALU.mult)
                    nc.gpsimd.tensor_tensor(SG[:, l, w, :, hd:DK], ssn[:, :, hd:DK], g[:, 0:hd].unsqueeze(1).to_broadcast([P, NT, hd]), ALU.mult)
                last = nc.gpsimd.tensor_scalar(bsub[:, l], bsub[:, l], 1.0 - LAM0[l], None, ALU.mult)
                last.then_inc(tables_ready, 1)

            def rsqrt(slot, rows, n, width):
                v, r = small_ss[0:rows, slot, 0:width], small_rs[0:rows, slot, 0:width]
                step(nc.gpsimd.tensor_scalar(v, v, 1.0 / n, EPS, ALU.mult, ALU.add))
                nc.gpsimd.tensor_tensor(r, v, half_neg[0:rows, 0:width], ALU.pow).then_inc(rs_ready, 1)

            def keys_and_history_out(l):
                for t in range(NT):
                    pool.wait_ge(rope_ready, 6 * l + t + 1)
                    dst = (k_p[l, 0, P * t:P * t + P] if t < 2 else k_s[l, 0]).rearrange("t h c d -> t (h c) d")
                    pool.dma_start(dst, krope[0:TILES[t][1], t, :, 0:DK]).then_inc(k_out, 16)
                pool.wait_ge(D_free, RD_.emptied(("hb", l, 1)))
                for dst, a in ((conv_p, SEQ), (conv_s, T + 2)):
                    for b in range(2):
                        with nc.allow_non_contiguous_dma(reason="two columns of history"):
                            pool.dma_start(dst[l, 0, :, b * P:b * P + P].rearrange("j p -> p j"), up[:, b, a:a + 2]).then_inc(cv_out, 16)

            def states_out(l):
                pool.wait_ge(D_free, RD_.emptied(("U", l, 4)))
                for dst, c in ((gla_p, 3), (gla_s, 4)):
                    for h in range(2):
                        pool.dma_start(dst[l, 0].rearrange("(r h) d e -> h d r e", h=2)[h], S[HW * h:HW * h + DK, c]).then_inc(st_out, 16)

            for l in range(DEPTH):
                for t, (t0, rows) in enumerate(TILES):
                    pool.wait_ge(rows_sq, 6 * l + t + 1)
                    rsqrt(rs_slot(l, "mix", t), rows, D, 1)
                if l:
                    pool.wait_ge(A_free, RA_.emptied(("pk", 0)))
                    pool.wait_ge(st_out, 16 * 4)
                    pool.wait_ge(cv_out, 16 * 4)
                    loads(l)
                for what, n, width in (("kc", DK, 8), ("qc", DK, 8), ("oa", DV, 4), ("oc", DV, 4)):
                    for t, (t0, rows) in enumerate(TILES):
                        pool.wait_ge(ss_ready, ss_count(l, what, t))
                        rsqrt(rs_slot(l, what, t), rows, n, width)
                    if what == "kc":
                        keys_and_history_out(l)
                    if what == "oa":
                        states_out(l)
                for t, (t0, rows) in enumerate(TILES):
                    pool.wait_ge(rows_sq, 6 * l + 3 + t + 1)
                    rsqrt(rs_slot(l, "ffn", t), rows, D, 1)

            for t, (t0, rows) in enumerate(TILES):
                pool.wait_ge(xhat_ready, 9 + t + 1)
                pool.dma_start(hx[t0:t0 + rows, :], xhat[0:rows, t, :]).then_inc(hx_out, 16)
            pool.wait_ge(hx_out, 16 * NT)
            pool.wait_ge(idx_ready, 1)
            pool.wait_ge(pairs_ready, 1)
            pairs = pool.value_load(npair[0:1, 0:1], min_val=NE // 2, max_val=NE // 2 * MAXB)

            def gather():
                pool.indirect_dma_start(out=xg[:], out_offset=None, in_=hx[:, :],
                                        in_offset=bass.IndirectOffsetOnAxis(ap=idc[:, 0:1], axis=0)).then_inc(xg_in, 16)

            nc.gpsimd.tensor_copy(idc[:, 0:1], idx[:, 0:1]).then_inc(idc_ready, 1)
            pool.wait_ge(idc_ready, 1)
            with pool.Fori(0, pairs * 2) as n:
                gather()
                pool.wait_ge(t_full, n * 9 + 2)
                pool.wait_ge(xg_in, n * 16 + 16)
                nc.gpsimd.tensor_copy(idc[:, 0:1], idx[:, bass.ds(n + 1, 1)]).then_inc(idc_ready, 1)
                pool.wait_ge(idc_ready, n + 2)
            gather()
            pool.wait_ge(pos_ready, NT)
            pool.wait_ge(rows_out, 1)
            for t, (t0, rows) in enumerate(TILES):
                for k in range(2):
                    if t:
                        pool.wait_ge(cmb_used, 2 * (t - 1) + k + 1)
                    pool.indirect_dma_start(out=cmb[0:rows, k, :], out_offset=None, in_=ybuf[:, :],
                                            in_offset=bass.IndirectOffsetOnAxis(ap=pos[0:rows, t, k:k + 1], axis=0)).then_inc(cmb_in[k], 16)

        @block.scalar
        def _(act):
            step = Steps(act, act_step)
            hs_n = [0]
            act.dma_start(const[:], A["const"]).then_inc(const_in, 16)
            act.dma_start(x[:, 0:2, :], A["x_prompt"][0].rearrange("(t p) d -> p t d", p=P)).then_inc(x_in, 16)
            act.dma_start(x[0:DEC, 2, :], A["x_sample"][0]).then_inc(x_in, 16)
            at = 0
            for name in ("g_q", "g_k", "lambda_q1", "lambda_k1", "lambda_q2", "lambda_k2", "g_gla", "g_sub"):
                n = DEPTH * A[name].shape[1]
                act.dma_start(brow[0:1, at:at + n], A[name].rearrange("l d -> (l d)").unsqueeze(0)).then_inc(brow_in, 16)
                at += n

            def norm_squares(i):
                for t, (t0, rows) in enumerate(TILES):
                    if i == 0:
                        act.wait_ge(x_in, 32)
                    else:
                        job = ("wo", i // 2, t) if i % 2 else ("dn", t)
                        act.wait_ge(A_free, RA_.emptied(job))
                        act.wait_ge(D_free, RD_.emptied(job))
                        if i % 2:
                            act.wait_ge(k_out, 16 * 3 * (i // 2 + 1))
                    nc.scalar.activation(xhat[0:rows, t, :], x[0:rows, t, :], ACT.Square,
                                         accum_out=small_ss[0:rows, rs_slot(i // 2, "ffn" if i % 2 else "mix", t), 0:1]).then_inc(rows_sq, 1)

            def norm_evacuate(i):
                for t, (t0, rows) in enumerate(TILES):
                    act.wait_ge(A_full, RA_.filled(("xt", i, t)))
                    b = RA_.bank(("xt", i, t)).rearrange("p (k n) -> p k n", k=4)
                    for k in range(4):
                        last = nc.scalar.activation(xT[:, k, t0:t0 + rows], b[:, k, 0:rows], ACT.Copy, scale=gcol(i)[:, k:k + 1])
                    last.then_inc(A_free, 1)

            norm_squares(0)
            act.wait_ge(A_full, RA_.filled(("par",)))
            nc.scalar.copy(pcol[:], RA_.bank(("par",))[:, 0:48]).then_inc(A_free, 1)
            act.wait_ge(A_full, RA_.filled(("bcast", 0)))
            nc.scalar.copy(bc[:, 0:480], RA_.bank(("bcast", 0))[:, 0:480]).then_inc(A_free, 1)
            act.wait_ge(A_free, 1)
            act.wait_ge(lam_exp, 1)
            nc.scalar.activation(lamt[:], lamt[:], ACT.Exp).then_inc(lam_exp, 1)

            for l in range(DEPTH):
                if l:
                    norm_squares(2 * l)
                norm_evacuate(2 * l)

                def copy_a(job, out, in_):
                    act.wait_ge(A_full, RA_.filled(job))
                    nc.scalar.copy(out, in_).then_inc(A_free, 1)

                copy_a(("ga", l), gaT, RA_.bank(("ga", l))[0:GR, 0:T])
                for t, (t0, rows) in enumerate(TILES):
                    copy_a(("qk", l, t), qkp[0:rows, t, :, 0:DK], RA_.bank(("qk", l, t))[0:rows, 0:384].rearrange("p (g d) -> p g d", g=8))
                for t, (t0, rows) in enumerate(TILES):
                    act.wait_ge(A_full, RA_.filled(("qkt", l, t)))
                    b = RA_.bank(("qkt", l, t)).rearrange("p (r n) -> p r n", r=4)
                    nc.scalar.copy(qr[:, :, t0:t0 + rows], b[:, 0:2, 0:rows])
                    nc.scalar.copy(kr[:, :, t0:t0 + rows], b[:, 2:4, 0:rows]).then_inc(A_free, 1)
                for b in range(2):
                    copy_a(("bb", l, b), bbs[:, b], RA_.bank(("bb", l, b))[:, 0:T])
                for b in range(2):
                    copy_a(("cb", l, b), cbs[:, b], RA_.bank(("cb", l, b))[:, 0:T])
                act.wait_ge(D_free, RD_.emptied(("gl", l, 1)))
                step(nc.scalar.activation(e1, z, ACT.Abs))
                step(nc.scalar.activation(e1, e1, ACT.Exp, scale=-1.0))
                nc.scalar.activation(e1, e1, ACT.Ln, bias=1.0).then_inc(ln_ready, 1)

                def squares(src, what, t, rows):
                    n = hs_n[0]
                    hs_n[0] += 1
                    if n >= 2:
                        act.wait_ge(ss_ready, n - 1)
                    nc.scalar.activation(sq[0:rows, n % 2, :], src, ACT.Square).then_inc(sq_ready, 1)

                def squares_of(what):
                    for t, (t0, rows) in enumerate(TILES):
                        act.wait_ge(D_full, RD_.filled((what, l, t)))
                        squares(RD_.bank((what, l, t))[0:rows, 0:384], what, t, rows)

                squares_of("kc")
                act.wait_ge(d_ready, 2 * l + 2)
                nc.scalar.activation(eq, d1, ACT.Exp, scale=1.0 / 16)
                nc.scalar.activation(ek, d1, ACT.Exp, scale=-1.0 / 16)
                nc.scalar.activation(eb, cum, ACT.Exp, scale=1.0 / 16)
                nc.scalar.activation(ed, ed, ACT.Exp, scale=1.0 / 16).then_inc(exps_ready, 1)
                squares_of("qc")
                copy_a(("pk", l), pkT[:], RA_.bank(("pk", l)).rearrange("p (h n) -> p h n", h=H))
                for t, (t0, rows) in enumerate(TILES):
                    copy_a(("kt", l, t), kT[:, :, t0:t0 + rows], RA_.bank(("kt", l, t)).rearrange("p (h n) -> p h n", h=H)[:, :, 0:rows])
                for t, (t0, rows) in enumerate(TILES):
                    if l and t == 0:
                        act.wait_ge(v_out, 16 * 2)
                    copy_a(("vc", l, t), vc[0:rows, t], RA_.bank(("vc", l, t))[0:rows, 0:384])
                for t, (t0, rows) in enumerate(TILES):
                    copy_a(("qt", l, t), qT[:, :, t0:t0 + rows], RA_.bank(("qt", l, t)).rearrange("p (h n) -> p h n", h=H)[:, :, 0:rows])
                for t, (t0, rows) in enumerate(TILES):
                    copy_a(("va", l, t), va[0:rows, t], RA_.bank(("va", l, t))[0:rows, 0:384])
                act.wait_ge(A_free, RA_.emptied(("vc", l, 2)))
                act.dma_start(v_p[l, 0].rearrange("(t p) h d -> p t (h d)", p=P), vc[:, 0:2]).then_inc(v_out, 16)
                act.dma_start(v_s[l, 0].rearrange("t h d -> t (h d)"), vc[0:DEC, 2]).then_inc(v_out, 16)
                for t, (t0, rows) in enumerate(TILES):
                    act.wait_ge(D_full, RD_.filled(("ra", l, t)))
                    nc.scalar.activation(sra[0:rows, t], RD_.bank(("ra", l, t))[0:rows, 0:384], ACT.Exp, scale=-1.0).then_inc(era_ready, 1)
                for t, (t0, rows) in enumerate(TILES):
                    copy_a(("kd", l, t), kdn[0:rows, t], RA_.bank(("kd", l, t)).rearrange("p (r n) -> p r n", r=2)[0:rows, :, 0:P])
                squares_of("oa")
                for n in range(NT * H + 2):
                    if n < NT * H:
                        t = n // H
                        rows, keys = TILES[t][1], [128, 256, 192][t]
                        act.wait_ge(nm_ready, NT * H * l + n + 1)
                        if n >= 2:
                            act.wait_ge(am_ready, NT * H * l + n - 1)
                        s = RS_.bank(("s", l, n)).rearrange("p (c k) -> p c k", c=2)
                        for c in range(2):
                            last = nc.scalar.activation(pe_[0:rows, n % 2, c, 0:keys], s[0:rows, c, 0:keys], ACT.Exp,
                                                        bias=nm[0:rows, n % 2, c:c + 1], scale=SC, accum_out=sm[0:rows, n % 2, c:c + 1])
                        last.then_inc(S_free, 1)
                    if 1 <= n <= NT * H:
                        m = n - 1
                        t = m // H
                        rows = TILES[t][1]
                        act.wait_ge(A_full, RA_.filled(("at", l, m)))
                        b = RA_.bank(("at", l, m)).rearrange("p (k n) -> p k n", k=4)
                        if t < 2:
                            nc.scalar.copy(aT[:, m % 2, 0:t + 1, :], b[:, 0:t + 1, :]).then_inc(A_free, 1)
                        else:
                            nc.scalar.copy(aT[:, m % 2, 0, 0:rows], b[:, 0, 0:rows])
                            nc.scalar.copy(aT[0:DEC, m % 2, 1, 0:rows], b[0:DEC, 1, 0:rows]).then_inc(A_free, 1)
                    if n in (H + 1, 2 * H + 1, 3 * H + 1):
                        t = n // H - 1
                        rows = TILES[t][1]
                        act.wait_ge(D_full, RD_.filled(("oc", l, t)))
                        squares(RD_.bank(("oc", l, t))[0:rows, 0:384], "oc", t, rows)
                for what, b0 in (("ya", 0), ("yc", 5)):
                    for t, (t0, rows) in enumerate(TILES):
                        copy_a((what, l, t), yT[:, b0:b0 + 3, t0:t0 + rows], RA_.bank((what, l, t)).rearrange("p (k n) -> p k n", k=4)[:, 0:3, 0:rows])

                norm_squares(2 * l + 1)
                norm_evacuate(2 * l + 1)
                outputs_left(act, l)
                if l == 0:
                    act.wait_ge(pool_zero, 6)
                    act.dma_start(ybuf[NE * P:, :].rearrange("(n p) d -> p n d", p=P),
                                  zeros[:].unsqueeze(1).to_broadcast([P, (MAXB - 1) * NE, D])).then_inc(ye_out, 16)
                    for f in range(FB):
                        act.wait_ge(A_full, RA_.filled(("g", f)))
                        if f >= 2:
                            act.wait_ge(D_free, RD_.emptied(("u", f - 2)))
                        nc.scalar.activation(sg[:, f % 2], RA_.bank(("g", f))[:, 0:T], ACT.Silu).then_inc(A_free, 1)

            for t, (t0, rows) in enumerate(TILES):
                act.wait_ge(gate_in, t + 1)
                nc.scalar.activation(gd[0:rows, t, 1:2], gd[0:rows, t, 0:1], ACT.Exp).then_inc(gate_out, 1)

            act.nop().then_inc(g_free, 1)
            act.nop().then_inc(y_free, 1)
            act.wait_ge(pairs_ready, 1)
            pairs = act.value_load(npair[0:1, 0:1], min_val=NE // 2, max_val=NE // 2 * MAXB)
            tb = [banks[4], banks[5]]

            def xg_hi(base, first):
                for k in range(KB):
                    if k % 4 == 0:
                        act.wait_ge(t_full, base + k // 4 + 1)
                    b = tb[(first + k // 4) % 2]
                    last = nc.scalar.activation(xgT_hi[:, k, :], b[:, 128 * (k % 4):128 * (k % 4) + 128], ACT.Copy, scale=gcol(3)[:, k:k + 1])
                    if k % 4 == 3:
                        last.then_inc(th_ready, 1)

            xg_hi(0, 0)
            with act.Fori(0, pairs) as ip:
                for i in range(2 * NP):
                    h, q = divmod(i, NP)
                    act.wait_ge(piece_full[i % PR], ip * (16 * 2 * NP // PR) + 16 * (i // PR + 1))
                    act.wait_ge(piece_used, ip * (2 * NP) + (i + 1))
                    nc.scalar.copy(split_hi[:, i % SR, :], raw[:, (i % PR) * PIECE:(i % PR + 1) * PIECE]).then_inc(hi_ready, 1)
                    if q % 4 == 0 and 1 <= q // 4 <= FC:
                        j = q // 4 - 1
                        m = FC * h + j
                        act.wait_ge(piece_used, ip * (2 * NP) + (NP * h + 4 * j + 2 + SR))
                        act.wait_ge(u_free, ip * (2 * FC) + max(m, 1))
                        nc.scalar.activation(hs[:, m % 2, :], banks[m % 2][:], ACT.Silu).then_inc(g_free, 1)
                    if q in HT_AT:
                        j = HT_AT.index(q)
                        n = 2 + 9 * h + j
                        act.wait_ge(t_full, ip * 18 + (n + 1))
                        nc.scalar.copy(hmT_hi[:, 4 * j:4 * j + 4, :].rearrange("p b n -> p (b n)"), tb[n % 2][:]).then_inc(th_ready, 1)
                    if q == X_AT:
                        xg_hi(ip * 18 + (9 * h + 9), 9 * h + 9)
                    if q == NP - 1:
                        act.wait_ge(piece_used, ip * (2 * NP) + (NP * (h + 1) + SR))
                        act.wait_ge(ye_out, ip * 32 + 16 * (h + 1))
                        nc.scalar.copy(ye[:, 0:512], banks[6][:])
                        nc.scalar.copy(ye[:, 512:1024], banks[7][:]).then_inc(y_free, 1)
                        act.wait_ge(y_free, ip * 2 + (h + 2))
                        act.dma_start(ybuf[bass.ds(ip * (2 * P) + h * P, P), :], ye[:]).then_inc(ye_out, 16)
            act.wait_ge(ye_out, pairs * 32 + 16)
            nc.scalar.copy(hs[0:1, 0, 0:1], ye[0:1, 0:1]).then_inc(rows_out, 1)
            for t in range(NT):
                act.wait_ge(cmb_used, 2 * (t + 1))
                act.dma_start(y_p[0, P * t:P * t + P] if t < 2 else y_s[0], x[0:TILES[t][1], t, :]).then_inc(y_out, 16)
            act.wait_ge(y_out, 16 * NT)
            act.wait_ge(k_out, 16 * NT * DEPTH)
            act.wait_ge(v_out, 16 * 2 * DEPTH)
            act.wait_ge(st_out, 16 * 4 * DEPTH)
            act.wait_ge(cv_out, 16 * 4 * DEPTH)
            act.wait_ge(hx_out, 16 * NT)

        @block.vector
        def _(dve):
            step = Steps(dve, dve_step)
            V = nc.vector
            dve.wait_ge(D_full, RD_.filled(("bcast", 1)))
            V.tensor_copy(bc[:, 480:960], RD_.bank(("bcast", 1))[:, 0:480]).then_inc(D_free, 1)
            dve.wait_ge(A_free, RA_.emptied(("bcast", 0)))
            dve.wait_ge(D_free, RD_.emptied(("bcast", 1)))
            V.memset(neglam[:], 0.0).then_inc(bcast_ready, 1)
            lp = t1[:, 0:4 * DK].rearrange("p (v l d) -> p v l d", v=2, l=DEPTH)
            step(V.tensor_tensor(lp[:, 0], bl[:, 0], bl[:, 1], ALU.mult))
            step(V.tensor_tensor(lp[:, 1], bl[:, 2], bl[:, 3], ALU.mult))
            V.tensor_reduce(lamt[:], lp, AX_X, ALU.add).then_inc(lam_exp, 1)
            dve.wait_ge(lam_exp, 2)
            step(V.tensor_tensor(neglam[:], lamt[:, 1], lamt[:, 0], ALU.subtract))
            for l in range(DEPTH):
                step(V.tensor_scalar(neglam[:, l:l + 1], neglam[:, l:l + 1], -LAM0[l], None, ALU.add))

            def norm(i):
                for t, (t0, rows) in enumerate(TILES):
                    s = rs_slot(i // 2, "ffn" if i % 2 else "mix", t)
                    dve.wait_ge(rs_ready, s + 1)
                    V.tensor_scalar(xhat[0:rows, t, :], x[0:rows, t, :], small_rs[0:rows, s, 0:1], None, ALU.mult).then_inc(xhat_ready, 1)
                for t, (t0, rows) in enumerate(TILES):
                    job = ("xt", i, t)
                    dve.wait_ge(D_full, RD_.filled(job))
                    if i == 0 and t == 0:
                        dve.wait_ge(A_free, RA_.emptied(("par",)))
                    V.tensor_tensor(xT[:, 4:8, t0:t0 + rows], RD_.bank(job).rearrange("p (k n) -> p k n", k=4)[:, :, 0:rows],
                                    gcol(i)[:, 4:8].unsqueeze(2).to_broadcast([P, 4, rows]), ALU.mult).then_inc(D_free, 1)

            def sum_squares(l, what, t, rows, groups):
                n = ss_count(l, what, t)
                dve.wait_ge(sq_ready, n)
                V.tensor_reduce(small_ss[0:rows, rs_slot(l, what, t), 0:groups],
                                sq[0:rows, (n - 1) % 2, :].rearrange("p (g d) -> p g d", g=groups), AX_X, ALU.add).then_inc(ss_ready, 1)

            def scaled(l, what, t, rows, groups, out):
                s = rs_slot(l, what, t)
                dve.wait_ge(rs_ready, s + 1)
                V.tensor_tensor(out[0:rows].rearrange("p (g d) -> p g d", g=groups),
                                RD_.bank((what, l, t))[0:rows, 0:384].rearrange("p (g d) -> p g d", g=groups),
                                small_rs[0:rows, s, 0:groups].unsqueeze(2).to_broadcast([rows, groups, 384 // groups]),
                                ALU.mult).then_inc(D_free, 1)
                dve.wait_ge(D_free, RD_.emptied((what, l, t)))

            for l in range(DEPTH):
                norm(2 * l)
                for r in range(2):
                    dve.wait_ge(D_full, RD_.filled(("gl", l, r)))
                    V.tensor_scalar(z[:, r], RD_.bank(("gl", l, r))[:, 0:T], bg2(l, r), None, ALU.add).then_inc(D_free, 1)
                    dve.wait_ge(D_free, RD_.emptied(("gl", l, r)))
                step(V.tensor_scalar(cum, z, 0.0, None, ALU.min))
                for b in range(2):
                    dve.wait_ge(D_full, RD_.filled(("hb", l, b)))
                    dve.wait_ge(A_free, RA_.emptied(("cb", l, b)))
                    if b == 0:
                        dve.wait_ge(pool_zero, 6)
                        dve.wait_ge(hist_in, 32 * (l + 1))
                    hbk = RD_.bank(("hb", l, b))
                    step(V.tensor_tensor(up[:, b, 2:2 + SEQ], hbk[:, 0:SEQ], cbs[:, b, 0:SEQ], ALU.mult))
                    V.tensor_tensor(up[:, b, SEQ + 4:T + 4], hbk[:, SEQ:T], cbs[:, b, SEQ:T], ALU.mult).then_inc(D_free, 1)
                dve.wait_ge(D_free, RD_.emptied(("hb", l, 1)))
                dve.wait_ge(ln_ready, l + 1)
                step(V.tensor_tensor(d1, cum, e1, ALU.subtract))
                for r in range(2):
                    step(V.tensor_tensor_scan(cum[:, r], C("scan"), d1[:, r], 0.0, ALU.mult, ALU.add))
                c5 = cum.rearrange("p r (c n) -> p (r c) n", n=CH)
                V.tensor_tensor(d1.rearrange("p r (c n) -> p (r c) n", n=CH), c5,
                                c5[:, :, CH // 2 - 1:CH // 2].to_broadcast([P, 10, CH]), ALU.subtract).then_inc(d_ready, 1)
                V.tensor_tensor(ed.rearrange("p r (c n) -> p (r c) n", n=CH),
                                c5[:, :, CH - 1:CH].to_broadcast([P, 10, CH]), c5, ALU.subtract).then_inc(d_ready, 1)

                def rope(what, out):
                    w = {"qc": 0, "kc": 1}[what]
                    hd = DK // 2
                    for t, (t0, rows) in enumerate(TILES):
                        sum_squares(l, what, t, rows, 8)
                    if what == "kc":
                        dve.wait_ge(tables_ready, l + 1)
                    for t, (t0, rows) in enumerate(TILES):
                        scaled(l, what, t, rows, 8, t1)
                        v = t1[0:rows].rearrange("p (g d) -> p g d", g=8)
                        a = t2[0:rows].rearrange("p (g d) -> p g d", g=8)
                        b = t3[0:rows].rearrange("p (g d) -> p g d", g=8)

                        def tab(x_, lo, hi):
                            return x_[0:rows, l, w, t, lo:hi].unsqueeze(1).to_broadcast([rows, 8, hi - lo])

                        V.tensor_tensor(a, v, tab(CG, 0, DK), ALU.mult)
                        V.tensor_tensor(b[:, :, 0:hd], v[:, :, hd:DK], tab(SG, 0, hd), ALU.mult)
                        step(V.tensor_tensor(b[:, :, hd:DK], v[:, :, 0:hd], tab(SG, hd, DK), ALU.mult))
                        V.tensor_tensor(out[0:rows, t, :, 0:DK], a, b, ALU.add).then_inc(rope_ready, 1)
                        dve.wait_ge(rope_ready, 6 * l + (0 if what == "kc" else 3) + t + 1)

                rope("kc", krope)
                dve.wait_ge(exps_ready, l + 1)
                dve.wait_ge(A_free, RA_.emptied(("qkt", l, 2)))
                V.tensor_tensor(ed, ed, kr, ALU.mult).then_inc(gk_ready, 1)
                qs = dict(scalar=SC, op0=ALU.mult, op1=ALU.mult)
                fl = lambda a: a.rearrange("p r n -> p (r n)")
                V.scalar_tensor_tensor(out=fl(qb), in0=fl(qr), in1=fl(eb), **qs)
                V.scalar_tensor_tensor(out=fl(eq), in0=fl(qr), in1=fl(eq), **qs)
                V.tensor_tensor(ek, ek, kr, ALU.mult).then_inc(gk_ready, 1)
                rope("qc", qrope)
                for b in range(2):
                    step(V.tensor_scalar(yv[:, b], up[:, b, 0:T + 2], wconv(l, 0, b), None, ALU.mult))
                    for j in (1, 2):
                        step(V.scalar_tensor_tensor(out=yv[:, b], in0=up[:, b, j:j + T + 2], scalar=wconv(l, j, b), in1=yv[:, b],
                                                    op0=ALU.mult, op1=ALU.add))
                V.tensor_tensor(yb[:, :, 0:SEQ], yv[:, :, 0:SEQ], bbs[:, :, 0:SEQ], ALU.mult)
                V.tensor_tensor(yb[:, :, SEQ:T], yv[:, :, SEQ + 2:T + 2], bbs[:, :, SEQ:T], ALU.mult).then_inc(conv_ready, 1)
                for t, (t0, rows) in enumerate(TILES):
                    dve.wait_ge(era_ready, NT * l + t + 1)
                    s = sra[0:rows, t]
                    step(V.tensor_scalar(s, s, 1.0, None, ALU.add))
                    step(V.reciprocal(s, s))
                    V.tensor_tensor(s, RD_.bank(("ra", l, t))[0:rows, 0:384], s, ALU.mult).then_inc(D_free, 1)
                msk = C("attm").bitcast(I32)
                for t, (t0, rows) in enumerate(TILES):
                    dve.wait_ge(D_full, RD_.filled(("att", l, t)))
                    V.copy_predicated(att[0:rows, t].rearrange("p h n -> p (h n)"), msk[0:rows], RD_.bank(("att", l, t))[0:rows, 0:H * CH]).then_inc(D_free, 1)
                ebc = eb.rearrange("p r (c n) -> p r c n", n=CH)
                for c in range(len(CHUNKS)):
                    dve.wait_ge(D_full, RD_.filled(("U", l, c)))
                    U = RD_.bank(("U", l, c))[:, 0:2 * DV].rearrange("p (r d) -> p r d", r=2)
                    if c == 0:
                        if l:
                            dve.wait_ge(st_out, 16 * 4)
                        V.tensor_copy(S[:, 0], U).then_inc(D_free, 1)
                    else:
                        prev = 5 if c == 4 else c - 1
                        if c == 4:
                            dve.wait_ge(s0_in, 32 * (l + 1))
                        step(V.scalar_tensor_tensor(out=S[:, c, 0], in0=S[:, prev, 0], scalar=ebc[:, 0, c, CH - 1:CH], in1=U[:, 0],
                                                    op0=ALU.mult, op1=ALU.add))
                        V.scalar_tensor_tensor(out=S[:, c, 1], in0=S[:, prev, 1], scalar=ebc[:, 1, c, CH - 1:CH], in1=U[:, 1],
                                               op0=ALU.mult, op1=ALU.add).then_inc(D_free, 1)
                    dve.wait_ge(D_free, RD_.emptied(("U", l, c)))

                def head_norm(what, t, rows, gain):
                    scaled(l, what, t, rows, H, t1)
                    return (t1[0:rows].rearrange("p (g d) -> p g d", g=H),
                            gain[0:rows, l].unsqueeze(1).to_broadcast([rows, H, DV]))

                for t, (t0, rows) in enumerate(TILES):
                    sum_squares(l, "oa", t, rows, H)
                for t, (t0, rows) in enumerate(TILES):
                    v, g = head_norm("oa", t, rows, bgla)
                    step(V.tensor_tensor(t2[0:rows].rearrange("p (g d) -> p g d", g=H), v, g, ALU.mult))
                    V.tensor_tensor(Ya[0:rows, t], t2[0:rows], sra[0:rows, t], ALU.mult).then_inc(ya_ready, 1)
                    dve.wait_ge(ya_ready, NT * l + t + 1)

                for n in range(NT * H + 3):
                    if n < NT * H:
                        t = n // H
                        rows, keys = TILES[t][1], [128, 256, 192][t]
                        dve.wait_ge(S_full, RS_.filled(("s", l, n)))
                        step(V.tensor_reduce(mx[0:rows, n % 2], RS_.bank(("s", l, n)).rearrange("p (c k) -> p c k", c=2)[0:rows, :, 0:keys], AX_X, ALU.max))
                        V.tensor_scalar(nm[0:rows, n % 2], mx[0:rows, n % 2], -SC, None, ALU.mult).then_inc(nm_ready, 1)
                    if 1 <= n <= NT * H:
                        m = n - 1
                        t = m // H
                        rows, keys = TILES[t][1], [128, 256, 192][t]
                        dve.wait_ge(S_free, RS_.emptied(("s", l, m)))
                        step(V.reciprocal(rc[0:rows], sm[0:rows, m % 2]))
                        step(V.tensor_tensor(rc2[0:rows], rc[0:rows, 1:2], neglam[0:rows, l:l + 1], ALU.mult))
                        if m >= 2:
                            dve.wait_ge(A_full, RA_.filled(("at", l, m - 2)))
                        step(V.tensor_scalar(atm[0:rows, 0:keys], pe_[0:rows, m % 2, 1, 0:keys], rc2[0:rows], None, ALU.mult))
                        V.scalar_tensor_tensor(out=am[0:rows, m % 2, 0:keys], in0=pe_[0:rows, m % 2, 0, 0:keys], scalar=rc[0:rows, 0:1],
                                               in1=atm[0:rows, 0:keys], op0=ALU.mult, op1=ALU.add).then_inc(am_ready, 1)
                        dve.wait_ge(am_ready, NT * H * l + m + 1)
                    if n in (H + 2, 2 * H + 2, 3 * H + 2):
                        t = n // H - 1
                        rows = TILES[t][1]
                        sum_squares(l, "oc", t, rows, H)
                        v, g = head_norm("oc", t, rows, bsub)
                        V.tensor_tensor(Yc[0:rows, t].rearrange("p (g d) -> p g d", g=H), v, g, ALU.mult).then_inc(yc_ready, 1)
                        dve.wait_ge(yc_ready, NT * l + t + 1)

                def add_to_x(job):
                    for t, (t0, rows) in enumerate(TILES):
                        for full, free, R, lo in ((A_full, A_free, RA_, 0), (D_full, D_free, RD_, 512)):
                            dve.wait_ge(full, R.filled(job(t)))
                            xs = x[0:rows, t, lo:lo + 512]
                            V.tensor_tensor(xs, xs, R.bank(job(t))[0:rows, :], ALU.add).then_inc(free, 1)

                add_to_x(lambda t: ("wo", l, t))
                norm(2 * l + 1)
                outputs_left(dve, l)
                if l == 0:
                    for f in range(FB):
                        dve.wait_ge(D_full, RD_.filled(("u", f)))
                        dve.wait_ge(A_free, RA_.emptied(("g", f)))
                        V.tensor_tensor(hT[:, f, :], sg[:, f % 2], RD_.bank(("u", f))[:, 0:T], ALU.mult).then_inc(D_free, 1)
                    add_to_x(lambda t: ("dn", t))

            i8 = C("iota8")
            for t, (t0, rows) in enumerate(TILES):
                dve.wait_ge(D_full, RD_.filled(("lg", t)))
                V.tensor_copy(lgs[0:rows, t], RD_.bank(("lg", t))[0:rows, 0:NE]).then_inc(D_free, 1)
                dve.wait_ge(D_free, RD_.emptied(("lg", t)))
                step(V.max(top[0:rows, t], lgs[0:rows, t]))
                step(V.max_index(topi[0:rows, t], top[0:rows, t], lgs[0:rows, t]))
                V.tensor_tensor(gd[0:rows, t, 0:1], top[0:rows, t, 1:2], top[0:rows, t, 0:1], ALU.subtract).then_inc(gate_in, 1)
                step(V.tensor_copy(topf[0:rows, t], topi[0:rows, t]))
                for k in range(2):
                    step(V.tensor_scalar(oh[0:rows, t, k], i8[0:rows], topf[0:rows, t, k:k + 1], None, ALU.is_equal))
                V.tensor_tensor(M[0:rows, t], oh[0:rows, t, 0], oh[0:rows, t, 1], ALU.add).then_inc(M_ready, 1)
                dve.wait_ge(M_ready, t + 1)
            for t, (t0, rows) in enumerate(TILES):
                dve.wait_ge(D_full, RD_.filled(("rk", t)))
                V.tensor_copy(rank[0:rows, t], RD_.bank(("rk", t))[0:rows, 0:NE]).then_inc(D_free, 1)
                dve.wait_ge(D_free, RD_.emptied(("rk", t)))
                step(V.scalar_tensor_tensor(out=rankm[0:rows, t], in0=rank[0:rows, t], scalar=1.0, in1=M[0:rows, t], op0=ALU.add, op1=ALU.mult))
                step(V.tensor_scalar(rankm[0:rows, t], rankm[0:rows, t], -1.0, None, ALU.add))
            dve.wait_ge(D_full, RD_.filled(("cnt",)))
            V.tensor_reduce(cntm[0:1, 0:1], RD_.bank(("cnt",))[0:1, 0:NE], AX_X, ALU.max).then_inc(D_free, 1)
            dve.wait_ge(D_free, RD_.emptied(("cnt",)))
            for b in range(1, MAXB):
                step(V.tensor_scalar(cntm[0:1, b:b + 1], cntm[0:1, 0:1], float(P * b), float(NE // 2), ALU.is_gt, ALU.mult))
            step(V.tensor_tensor(cntm[0:1, 3:4], cntm[0:1, 1:2], cntm[0:1, 2:3], ALU.add))
            step(V.tensor_copy(npair[0:1, 1:2], cntm[0:1, 3:4]))
            V.tensor_scalar(npair[0:1, 0:1], cntm[0:1, 3:4], float(NE // 2), None, ALU.add).then_inc(pairs_ready, 1)
            step(V.memset(idx[:], 0))
            for e in range(NE):
                if e >= 2:
                    dve.wait_ge(G_used, e - 1)
                for t, (t0, rows) in enumerate(TILES):
                    last = V.tensor_scalar(G[0:rows, e % 2, t], C("slot", rows), rankm[0:rows, t, e:e + 1], None, ALU.is_equal)
                last.then_inc(G_ready, 1)
            dve.wait_ge(D_full, RD_.filled(("idx",)))
            V.tensor_copy(idx[:, 0:MAXB * NE], RD_.bank(("idx",))[:, 0:MAXB * NE]).then_inc(idx_ready, 1)

            for t, (t0, rows) in enumerate(TILES):
                for k in range(2):
                    step(V.tensor_tensor(rtmp[0:rows, k], oh[0:rows, t, k], rank[0:rows, t], ALU.mult))
                    step(V.tensor_reduce(rk2[0:rows, t, k:k + 1], rtmp[0:rows, k], AX_X, ALU.add))
                step(V.tensor_scalar(posf[0:rows, t], topf[0:rows, t, 0:2], float(P), None, ALU.mult))
                step(V.tensor_tensor(posf[0:rows, t], posf[0:rows, t], rk2[0:rows, t], ALU.add))
                for b in range(1, MAXB):
                    step(V.tensor_scalar(ov[0:rows], rk2[0:rows, t], float(P * b), float(NE * P - P), ALU.is_ge, ALU.mult))
                    step(V.tensor_tensor(posf[0:rows, t], posf[0:rows, t], ov[0:rows], ALU.add))
                V.tensor_copy(pos[0:rows, t], posf[0:rows, t]).then_inc(pos_ready, 1)
                dve.wait_ge(gate_out, t + 1)
                step(V.tensor_scalar(gd[0:rows, t, 0:1], gd[0:rows, t, 1:2], 1.0, None, ALU.add))
                step(V.reciprocal(gd[0:rows, t, 2:3], gd[0:rows, t, 0:1]))
                step(V.tensor_tensor(gd[0:rows, t, 3:4], gd[0:rows, t, 1:2], gd[0:rows, t, 2:3], ALU.mult))

            dve.nop().then_inc(u_free, 1)
            dve.nop().then_inc(lo_ready, PR)
            dve.wait_ge(pairs_ready, 1)
            pairs = dve.value_load(npair[0:1, 0:1], min_val=NE // 2, max_val=NE // 2 * MAXB)
            tb = [banks[4], banks[5]]

            def xg_lo(first, base):
                for k in range(KB):
                    if k % 4 == 0:
                        dve.wait_ge(th_ready, base + (first + k // 4 + 1))
                    b = tb[(first + k // 4) % 2]
                    last = V.scalar_tensor_tensor(out=xgT_lo[:, k, :], in0=b[:, 128 * (k % 4):128 * (k % 4) + 128], scalar=gcol(3)[:, k:k + 1],
                                                  in1=xgT_hi[:, k, :].bitcast(F32), op0=ALU.mult, op1=ALU.subtract)
                    if k % 4 == 3:
                        last.then_inc(t_free, 1)

            xg_lo(0, 0)
            with dve.Fori(0, pairs) as ip:
                for i in range(2 * NP):
                    h, q = divmod(i, NP)
                    dve.wait_ge(hi_ready, ip * (2 * NP) + (i + 1))
                    V.tensor_tensor(split_lo[:, i % SR, :], raw[:, (i % PR) * PIECE:(i % PR + 1) * PIECE],
                                    split_hi[:, i % SR, :].bitcast(F32), ALU.subtract).then_inc(lo_ready, 1)
                    if q % 4 == 2 and 1 <= q // 4 <= FC:
                        j = q // 4 - 1
                        m = FC * h + j
                        dve.wait_ge(piece_used, ip * (2 * NP) + (NP * h + 4 * j + 4 + SR))
                        dve.wait_ge(g_free, ip * (2 * FC) + (m + 2))
                        dve.wait_ge(t_full, ip * 18 + (2 + 9 * h + max(j - 1, 0)))
                        V.tensor_tensor(hm[:, m % 2, :], hs[:, m % 2, :], banks[2 + m % 2][:], ALU.mult).then_inc(u_free, 1)
                    if q in HT_AT:
                        j = HT_AT.index(q)
                        n = 2 + 9 * h + j
                        dve.wait_ge(th_ready, ip * 18 + (n + 1))
                        V.tensor_tensor(hmT_lo[:, 4 * j:4 * j + 4, :].rearrange("p b n -> p (b n)"), tb[n % 2][:],
                                        hmT_hi[:, 4 * j:4 * j + 4, :].rearrange("p b n -> p (b n)").bitcast(F32), ALU.subtract).then_inc(t_free, 1)
                    if q == X_AT:
                        xg_lo(9 * h + 9, ip * 18)

            for t, (t0, rows) in enumerate(TILES):
                for k in range(2):
                    dve.wait_ge(cmb_in[k], 16 * (t + 1))
                    xs = x[0:rows, t, :]
                    V.scalar_tensor_tensor(out=xs, in0=cmb[0:rows, k, :], scalar=gd[0:rows, t, 2 + k:3 + k], in1=xs,
                                           op0=ALU.mult, op1=ALU.add).then_inc(cmb_used, 1)
                    dve.wait_ge(cmb_used, 2 * t + k + 1)

        @block.tensor
        def _(pe):
            TE = nc.tensor
            owed = [0]
            step = Steps(pe, pe_step)

            def issue(ins):
                if owed[0]:
                    ins.then_inc(unit_used, 1)
                    owed[0] -= 1
                return ins

            def mm(out, lhsT, rhs, start, stop):
                return issue(TE.matmul(out, lhsT, rhs, start=start, stop=stop))

            def tr(out, in_, rows):
                return issue(TE.transpose(out, in_, ident[0:rows, 0:rows]))

            def unit(u):
                n = UNIT[u]
                pe.wait_ge(ring_full[n % RING], 16 * (n // RING + 1))
                return ring[:, n % RING, :]

            def done():
                assert owed[0] == 0
                owed[0] = 1

            pe.wait_ge(const_in, 16)
            pe.wait_ge(prow_in, 64)
            tr(RA_.begin(pe, ("par",))[:, 0:48], prow, 48).then_inc(A_full, 1)
            pe.wait_ge(brow_in, 16 * 8)
            for i, (R, full) in enumerate(((RA_, A_full), (RD_, D_full))):
                mm(R.begin(pe, ("bcast", i))[:, 0:480], C("ones", 1), brow[0:1, 480 * i:480 * i + 480], True, True).then_inc(full, 1)

            def norm(i):
                for t, (t0, rows) in enumerate(TILES):
                    pe.wait_ge(xhat_ready, 3 * i + t + 1)
                    for R, full, k0 in ((RA_, A_full, 0), (RD_, D_full, 4)):
                        b = R.begin(pe, ("xt", i, t))
                        for k in range(4):
                            last = tr(b[:, 128 * k:128 * k + rows], xhat[0:rows, t, 128 * (k0 + k):128 * (k0 + k) + 128], rows)
                        last.then_inc(full, 1)

            def xT_ready(i):
                pe.wait_ge(A_free, RA_.emptied(("xt", i, 2)))
                pe.wait_ge(D_free, RD_.emptied(("xt", i, 2)))

            for l in range(DEPTH):
                norm(2 * l)
                xT_ready(2 * l)
                if l == 0:
                    pe.wait_ge(w_small, 16 * 7)

                def features(R, full, job, lhs, rows):
                    b = R.begin(pe, job)[0:rows, 0:T]
                    for k in range(KB):
                        last = mm(b, lhs(k), xT[:, k, :], k == 0, k == KB - 1)
                    last.then_inc(full, 1)

                def tokens(R, full, what):
                    w = unit((what, l))
                    for t, (t0, rows) in enumerate(TILES):
                        b = R.begin(pe, (what, l, t))[0:rows, 0:384]
                        for k in range(KB):
                            last = mm(b, xT[:, k, t0:t0 + rows], w[:, 384 * k:384 * k + 384], k == 0, k == KB - 1)
                        last.then_inc(full, 1)
                    done()

                def heads_T(job, t, src):
                    rows = TILES[t][1]
                    b = RA_.begin(pe, job)
                    for h in range(H):
                        last = tr(b[:, 128 * h:128 * h + rows], src[0:rows, 2 * h:2 * h + 2, :].rearrange("p c d -> p (c d)"), rows)
                    last.then_inc(A_full, 1)

                features(RA_, A_full, ("ga", l), lambda k: wga[:, l, k, :], GR)
                tokens(RA_, A_full, "qk")
                for t in range(NT):
                    pe.wait_ge(A_free, RA_.emptied(("qk", l, t)))
                    heads_T(("qkt", l, t), t, qkp[:, t])
                w = unit(("bc", l))
                for i, name in enumerate(("bb", "cb")):
                    for b in range(2):
                        features(RA_, A_full, (name, l, b), lambda k, o=256 * i + 128 * b, w=w: w[:, 512 * k + o:512 * k + o + 128], P)
                done()
                for r in range(2):
                    pe.wait_ge(A_free, RA_.emptied(("ga", l)))
                    TE.matmul(RD_.begin(pe, ("gl", l, r))[:, 0:T], wg2[:, l, r, :], gaT, start=True, stop=True).then_inc(D_full, 1)
                w = unit(("hb", l))
                for b in range(2):
                    features(RD_, D_full, ("hb", l, b), lambda k, o=128 * b, w=w: w[:, 256 * k + o:256 * k + o + 128], P)
                done()

                tokens(RD_, D_full, "kc")
                tokens(RD_, D_full, "qc")
                pe.wait_ge(past_in, 32 * (l + 1))
                heads_T(("pk", l), 0, pkr)
                for t in range(NT):
                    pe.wait_ge(rope_ready, 6 * l + t + 1)
                    heads_T(("kt", l, t), t, krope[:, t])
                tokens(RA_, A_full, "vc")
                for t in range(NT):
                    pe.wait_ge(rope_ready, 6 * l + 3 + t + 1)
                    heads_T(("qt", l, t), t, qrope[:, t])
                tokens(RA_, A_full, "va")
                tokens(RD_, D_full, "ra")
                pe.wait_ge(gk_ready, 2 * l + 2)
                for t, (t0, rows) in enumerate(TILES):
                    b = RA_.begin(pe, ("kd", l, t))
                    for r in range(2):
                        last = tr(b[0:rows, 256 * r:256 * r + 128], ed[:, r, t0:t0 + rows], P)
                    last.then_inc(A_full, 1)
                for t, (t0, rows) in enumerate(TILES):
                    b = RD_.begin(pe, ("att", l, t))
                    for q0 in (0, HW):
                        for c in range(rows // CH):
                            a, p0 = t0 + CH * c, CH * c
                            for r in range(2):
                                o = CH * (2 * r + q0 // HW)
                                last = mm(b[p0:p0 + CH, o:o + CH], ek[q0:q0 + DK, r, a:a + CH], eq[q0:q0 + DK, r, a:a + CH], True, True)
                        if q0 == 0:
                            step(last)
                    last.then_inc(D_full, 1)
                pe.wait_ge(A_free, RA_.emptied(("kd", l, 2)))
                for c, (t, p0) in enumerate(CHUNKS):
                    b = RD_.begin(pe, ("U", l, c))
                    for h in range(H):
                        r, q0 = h // 2, HW * (h % 2)
                        last = mm(b[q0:q0 + HW, DV * r:DV * r + DV], kdn[p0:p0 + CH, t, r, q0:q0 + HW], va[p0:p0 + CH, t, DV * h:DV * h + DV], True, True)
                    last.then_inc(D_full, 1)
                for t, (t0, rows) in enumerate(TILES):
                    b = RD_.begin(pe, ("oa", l, t))
                    if t == 0:
                        pe.wait_ge(D_free, RD_.emptied(("att", l, 2)))
                    pe.wait_ge(D_free, RD_.emptied(("U", l, {0: 0, 1: 2, 2: 4}[t])))
                    work = {0: [], HW: []}
                    late = []
                    for c in range(rows // CH):
                        p0, a = CH * c, t0 + CH * c
                        before = 5 if t == 2 else 2 * t + c - 1
                        inner = [(b[p0:p0 + CH, DV * h:DV * h + DV], att[p0:p0 + CH, t, h, :], va[p0:p0 + CH, t, DV * h:DV * h + DV]) for h in range(H)]
                        work[p0] += [(m, i == 0, c) for i, m in enumerate(inner)]
                        if before >= 0:
                            for h in range(H):
                                r, q0 = h // 2, HW * (h % 2)
                                m = (b[p0:p0 + CH, DV * h:DV * h + DV], qb[q0:q0 + DK, r, a:a + CH], S[q0:q0 + DK, before, r, :])
                                (late if q0 < p0 else work[q0]).append((m, False, c))
                    groups = [g for g in (work[0], work[HW], late) if g]
                    for i, g in enumerate(groups):
                        for k, ((o, lhsT, rhs), first, c) in enumerate(g):
                            left = [x[2] for x in g[k + 1:]] + [x[2] for later in groups[i + 1:] for x in later]
                            last = mm(o, lhsT, rhs, first, c not in left)
                        if i < len(groups) - 1:
                            step(last)
                    last.then_inc(D_full, 1)

                for n in range(NT * H + 2):
                    if n < NT * H:
                        t, h = divmod(n, H)
                        t0, rows = TILES[t]
                        if n == 0:
                            pe.wait_ge(A_free, RA_.emptied(("qt", l, 2)))
                        b = RS_.begin(pe, ("s", l, n)).rearrange("p (c k) -> p c k", c=2)
                        for c in range(2):
                            if c:
                                step(last)
                            q0 = HW * c
                            q = qT[q0:q0 + DK, h, t0:t0 + rows]
                            if t < 2:
                                keys = P * (t + 1)
                                mm(b[:, c, 0:keys], q, kT[q0:q0 + DK, h, 0:keys], True, False)
                                last = mm(b[:, c, keys - CH:keys], C("rowsel")[q0:q0 + 1], C("neg")[q0:q0 + 1], False, True)
                            else:
                                mm(b[0:rows, c, 0:PAST], q, pkT[q0:q0 + DK, h, :], True, True)
                                last = mm(b[0:rows, c, PAST:PAST + DEC], q, kT[q0:q0 + DK, h, SEQ:T], True, True)
                        last.then_inc(S_full, 1)
                    if 1 <= n <= NT * H:
                        m = n - 1
                        t = m // H
                        rows = TILES[t][1]
                        pe.wait_ge(am_ready, NT * H * l + m + 1)
                        b = RA_.begin(pe, ("at", l, m))
                        for i, nk in enumerate([[128], [128, 128], [128, 64]][t]):
                            last = tr(b[0:nk, 128 * i:128 * i + rows], am[0:rows, m % 2, 128 * i:128 * i + nk], rows)
                        last.then_inc(A_full, 1)
                    if n >= 2:
                        m = n - 2
                        t, h = divmod(m, H)
                        rows = TILES[t][1]
                        pe.wait_ge(A_free, RA_.emptied(("at", l, m)))
                        b = RD_.begin(pe, ("oc", l, t)) if h == 0 else RD_.bank(("oc", l, t))
                        vs = [[(vc, 0)], [(vc, 0), (vc, 1)], [(pv, l), (vc, 2)]][t]
                        for i, (v, at) in enumerate(vs):
                            nk = DEC if t == 2 and i == 1 else P
                            last = mm(b[0:rows, DV * h:DV * h + DV], aT[0:nk, m % 2, i, 0:rows], v[0:nk, at, DV * h:DV * h + DV], i == 0, i == len(vs) - 1)
                        if h == H - 1:
                            last.then_inc(D_full, 1)

                for what, src, ready in (("ya", Ya, ya_ready), ("yc", Yc, yc_ready)):
                    for t, (t0, rows) in enumerate(TILES):
                        pe.wait_ge(ready, NT * l + t + 1)
                        b = RA_.begin(pe, (what, l, t))
                        for k in range(3):
                            last = tr(b[:, 128 * k:128 * k + rows], src[0:rows, t, 128 * k:128 * k + 128], rows)
                        last.then_inc(A_full, 1)

                def down(job, blocks, lhs, unit_of):
                    bs = {}
                    for t in range(NT):
                        bs[t, 0] = RA_.begin(pe, job(t))
                        bs[t, 1] = RD_.begin(pe, job(t))
                    for b in range(blocks):
                        if b % 4 == 0:
                            w = unit(unit_of(b // 4))
                        for t, (t0, rows) in enumerate(TILES):
                            for i, full in enumerate((A_full, D_full)):
                                o = 1024 * (b % 4) + 512 * i
                                last = mm(bs[t, i][0:rows, :], lhs(b, t0, rows), w[:, o:o + 512], b == 0, b == blocks - 1)
                                if b == blocks - 1:
                                    last.then_inc(full, 1)
                        if b % 4 == 3 or b == blocks - 1:
                            done()

                pe.wait_ge(A_free, RA_.emptied(("yc", l, 2)))
                pe.wait_ge(conv_ready, l + 1)
                down(lambda t: ("wo", l, t), KB,
                     lambda b, t0, rows: (yb[:, b - 3, t0:t0 + rows] if b in (3, 4) else yT[:, b, t0:t0 + rows]),
                     lambda j: ("wo", l, j))

                norm(2 * l + 1)
                xT_ready(2 * l + 1)
                if l == 0:
                    for f in range(FB):
                        n = min(512, FF - 512 * (f // 4))
                        for what, R, full in (("g", RA_, A_full), ("u", RD_, D_full)):
                            w = unit((what, f // 4))
                            features(R, full, (what, f), lambda k, w=w, o=128 * (f % 4): w[:, n * k + o:n * k + o + 128], P)
                            if f % 4 == 3 or f == FB - 1:
                                done()
                    pe.wait_ge(D_free, RD_.emptied(("u", FB - 1)))
                    down(lambda t: ("dn", t), FB, lambda b, t0, rows: hT[:, b, t0:t0 + rows], lambda j: ("d", j))

            for t, (t0, rows) in enumerate(TILES):
                b = RD_.begin(pe, ("lg", t))
                for k in range(KB):
                    last = mm(b[0:rows, 0:NE], xT[:, k, t0:t0 + rows], wr[:, k, :], k == 0, k == KB - 1)
                last.then_inc(D_full, 1)
            for t, (t0, rows) in enumerate(TILES):
                pe.wait_ge(M_ready, t + 1)
                b = RD_.begin(pe, ("rk", t))[0:rows, 0:NE]
                for s in range(t):
                    mm(b, C("ones")[:, 0:rows], M[:, s, :], s == 0, False)
                mm(b, C("tri", rows)[:, 0:rows], M[0:rows, t, :], t == 0, True).then_inc(D_full, 1)
            b = RD_.begin(pe, ("cnt",))[:, 0:NE]
            for t, (t0, rows) in enumerate(TILES):
                last = mm(b, C("ones", rows), M[0:rows, t, :], t == 0, t == NT - 1)
            last.then_inc(D_full, 1)
            b = RD_.begin(pe, ("idx",))
            for e in range(NE):
                pe.wait_ge(G_ready, e + 1)
                for s in range(MAXB):
                    for t, (t0, rows) in enumerate(TILES):
                        last = mm(b[:, NE * s + e:NE * s + e + 1], G[0:rows, e % 2, t, P * s:P * s + P], C("tok", rows)[:, t:t + 1], t == 0, t == NT - 1)
                if e < NE - 1:
                    last.then_inc(G_used, 1)
            last.then_inc(D_full, 1)
            assert owed[0] == 0

            pe.wait_ge(A_free, RA_.count)
            pe.wait_ge(D_free, RD_.count - 1)
            pe.wait_ge(idx_ready, 1)
            pe.wait_ge(pairs_ready, 1)
            pairs = pe.value_load(npair[0:1, 0:1], min_val=NE // 2, max_val=NE // 2 * MAXB)
            tb = [banks[4], banks[5]]
            pe.nop().then_inc(piece_used, SR)

            def xg_T(first, base):
                for i in range(2):
                    if base is not None:
                        pe.wait_ge(t_free, base + (first + i - 1))
                    for k in range(4):
                        last = tr(tb[(first + i) % 2][:, 128 * k:128 * k + 128], xg[:, 512 * i + 128 * k:512 * i + 128 * k + 128], P)
                    last.then_inc(t_full, 1)

            pe.wait_ge(xg_in, 16)
            xg_T(0, None)
            with pe.Fori(0, pairs) as ip:
                for i in range(2 * NP):
                    h, q = divmod(i, NP)
                    hi, lo = split_hi[:, i % SR, :], split_lo[:, i % SR, :]
                    j, half = q // 2, q % 2
                    if q == 0:
                        pe.wait_ge(t_free, ip * 18 + (2 + 9 * h))
                    if j < 2 * FC and half == 0:
                        m = FC * h + j // 2
                        pe.wait_ge(u_free if j % 2 else g_free, ip * (2 * FC) + max(m, 1))
                    if q == 4 * FC:
                        pe.wait_ge(y_free, ip * 2 + (h + 1))
                    if q >= 4 * FC and half == 0:
                        pe.wait_ge(t_free, ip * 18 + (2 + 9 * h + j - 2 * FC + 1))
                    pe.wait_ge(lo_ready, ip * (2 * NP) + (i + 1 + PR))
                    if j < 2 * FC:
                        o = banks[2 * (j % 2) + (FC * h + j // 2) % 2][:]
                        for k in range(4):
                            kk = 4 * half + k
                            c = slice(512 * k, 512 * k + 512)
                            TE.matmul(o, xgT_hi[:, kk, :], hi[:, c], start=kk == 0, stop=False)
                            TE.matmul(o, xgT_hi[:, kk, :], lo[:, c], start=False, stop=False)
                            last = TE.matmul(o, xgT_lo[:, kk, :], hi[:, c], start=False, stop=kk == KB - 1)
                    else:
                        for k in range(2):
                            b = 4 * (j - 2 * FC) + 2 * half + k
                            cs = [slice(1024 * k + 512 * n, 1024 * k + 512 * n + 512) for n in range(2)]
                            for n in range(2):
                                TE.matmul(banks[6 + n][:], hmT_hi[:, b, :], hi[:, cs[n]], start=b == 0, stop=False)
                                TE.matmul(banks[6 + n][:], hmT_hi[:, b, :], lo[:, cs[n]], start=False, stop=False)
                            for n in range(2):
                                last = TE.matmul(banks[6 + n][:], hmT_lo[:, b, :], hi[:, cs[n]], start=False, stop=b == FEB - 1)
                    last.then_inc(piece_used, 1)
                    if q in [a - 4 for a in HT_AT]:
                        c = HT_AT.index(q + 4)
                        m, n = FC * h + c, 2 + 9 * h + c
                        pe.wait_ge(u_free, ip * (2 * FC) + (m + 2))
                        pe.wait_ge(t_free, ip * 18 + (n - 1))
                        for k in range(4):
                            last = TE.transpose(tb[n % 2][:, 128 * k:128 * k + 128], hm[:, m % 2, 128 * k:128 * k + 128], ident)
                        last.then_inc(t_full, 1)
                    if q == X_AT - 4:
                        pe.wait_ge(xg_in, ip * 32 + 16 * (h + 2))
                        xg_T(9 * h + 9, ip * 18)


_INS = ['x_prompt', 'x_sample', 'state_gla', 'state_conv', 'cache_k', 'cache_v', 'g_mix', 'w_in', 'w_g2', 'b_g2', 'g_gla',
        'w_conv', 'g_q', 'g_k', 'lambda_q1', 'lambda_k1', 'lambda_q2', 'lambda_k2', 'g_sub', 'w_out', 'g_ffn',
        'ffn_w_gate', 'ffn_w_up', 'ffn_w_down', 'w_router', 'moe_w_gate', 'moe_w_up', 'moe_w_down']
_OUTS = [(1, SEQ, D), (1, DEC, D), (DEPTH, 1, SEQ, H, 2, DK), (DEPTH, 1, SEQ, H, DV), (DEPTH, 1, H, DK, DV), (DEPTH, 1, 2, 256),
         (DEPTH, 1, DEC, H, 2, DK), (DEPTH, 1, DEC, H, DV), (DEPTH, 1, H, DK, DV), (DEPTH, 1, 2, 256)]


def _constants():
    c = np.zeros((P, CONST_W), np.float32)

    def at(name):
        a, w = CONST[name]
        return c[:, a:a + w]

    p = np.arange(P)
    at("ident")[:] = np.eye(P)
    at("tri")[:] = p[:, None] < p[None, :]
    at("ones")[:] = 1
    at("scan")[:] = np.arange(T) % CH != 0
    half = DK // 2
    freq = np.float32(10000.0) ** (-np.arange(half, dtype=np.float32) / np.float32(half))
    for t, (t0, rows) in enumerate(TILES):
        position = (t0 + p if t < 2 else PAST + p).astype(np.float32)
        angle = position[:, None] * freq[None, :]
        cos, sin = np.cos(angle), np.sin(angle)
        at("cc")[:, t * DK:(t + 1) * DK] = np.concatenate([cos, cos], 1)
        at("ss")[:, t * DK:(t + 1) * DK] = np.concatenate([-sin, sin], 1)
        at("tok")[:, t] = t0 + p
    at("iota8")[:] = np.arange(8)
    at("slot")[:] = np.arange(MAXB * P)
    at("attm")[:] = np.tile((p % CH)[:, None] <= np.arange(CH)[None, :], (1, H))
    at("rowsel")[:] = p < CH
    at("neg")[:] = -1e30
    return c


def kernel(**inputs):
    import concourse.bacc as _bacc
    from concourse.bass_utils import run_bass_kernel_spmd as _run

    nc = _bacc.Bacc("TRN2", target_bir_lowering=False, num_devices=1)
    arrays = {name: np.ascontiguousarray(inputs[name]) for name in _INS}
    arrays["const"] = _constants()
    aps = {name: nc.dram_tensor(name, a.shape, mybir.dt.from_np(a.dtype), kind="ExternalInput").ap() for name, a in arrays.items()}
    outs = [nc.dram_tensor(f"out_{i}", shape, F32, kind="ExternalOutput").ap() for i, shape in enumerate(_OUTS)]
    build(nc, aps, outs)
    r = _run(nc, [arrays], core_ids=[0])
    return tuple(r.results[0][f"out_{i}"] for i in range(len(_OUTS)))
```

```python
from contextlib import ExitStack

import numpy as np
import concourse.bass as bass
from concourse import mybir

F32 = mybir.dt.float32
FR = mybir.dt.float32r
BF = mybir.dt.bfloat16
I32 = mybir.dt.int32
U32 = mybir.dt.uint32
ALU = mybir.AluOpType
ACT = mybir.ActivationFunctionType
AX_X = mybir.AxisListType.X

P = 128
D = 1024
KB = D // P
SEQ, DEC, PAST = 256, 64, 128
T = SEQ + DEC
TILES = [(0, 128), (128, 128), (256, 64)]
NT = len(TILES)
CH = 64
CHUNKS = [(0, 0), (0, 64), (1, 0), (1, 64), (2, 0)]
H = 4
DK = 48
DV = 96
HW = 64
GR = 16
DEPTH = 2
EPS = 1e-6
FF = 2816
FB = FF // P
NE = 8
FE = 3584
FC = FE // 512
FEB = FE // P
MAXB = 3
LAM0 = [0.8 - 0.6 * float(np.exp(-0.3 * l)) for l in range(DEPTH)]
SC = DK ** -0.5

QA, KA, VA, GA, RA = 0, 192, 384, 768, 784
BB, CB, HB = 1168, 1424, 1680
QC, KC, VC = 1936, 2320, 2704

CONST = {}
_at = 0
for _name, _w in [("ident", 128), ("tri", 128), ("ones", 128), ("scan", T), ("cc", NT * DK), ("ss", NT * DK),
                  ("tok", NT), ("iota8", 8), ("slot", MAXB * P), ("attm", H * CH), ("rowsel", P), ("neg", CH)]:
    CONST[_name] = (_at, _w)
    _at += _w
CONST_W = _at

RING = 3
SLOT = KB * 512

UNITS = []
for _l in range(DEPTH):
    UNITS += [("qk", _l), ("bc", _l), ("hb", _l), ("kc", _l), ("qc", _l), ("vc", _l), ("va", _l), ("ra", _l),
              ("wo", _l, 0), ("wo", _l, 1)]
    if _l == 0:
        for _j in range((FB + 3) // 4):
            UNITS += [("g", _j), ("u", _j)]
        UNITS += [("d", _c, _j) for _c in range(2) for _j in range((FB + 7) // 8)]
UNIT = {u: n for n, u in enumerate(UNITS)}


def is_dense(u):
    return u[0] in ("g", "u", "d")


def plain_units(n):
    return sum(not is_dense(u) for u in UNITS[:n])


CUT = KB * P
CUTS = []
for _f in range(FB):
    CUTS += [(("g", _f // 4), "g", _f), (("u", _f // 4), "u", _f)]
for _c in range(2):
    CUTS += [(("d", _c, _m // 4), "d", (_c, _m)) for _m in range(FB // 2)]
CR = 3
LAST_CUT = {u: q for q, (u, _k, _w) in enumerate(CUTS)}
DOWN0 = 2 * FB
HALF = FB // 2
DOWN_BANKS = [[("A", 4 * _c), ("D", 4 * _c + 2), ("A", 4 * _c + 1), ("D", 4 * _c + 3)] for _c in range(2)]
UE = 3 * FC
PIECE = SLOT // 2
NP = 2 * UE
PR = 7
SR = 3
assert 2 * NP % PR == 0 and 2 * NP % SR == 0 and PR * PIECE >= RING * SLOT


HT_AT = [4 * _j + 11 for _j in range(FC - 1)] + [4 * FC + 7]
X_AT = NP - 3

JOBS_A, JOBS_D, JOBS_S = [], [], []


def _norm_jobs(i):
    for t in range(NT):
        JOBS_A.append(("xt", i, t))
        JOBS_D.append(("xt", i, t))


JOBS_A += [("par",), ("bcast", 0)]
JOBS_D += [("bcast", 1)]
for _l in range(DEPTH):
    _norm_jobs(2 * _l)
    JOBS_A += [("ga", _l)] + [("qk", _l, t) for t in range(NT)] + [("qkt", _l, t) for t in range(NT)]
    JOBS_A += [("bb", _l, 0), ("bb", _l, 1), ("cb", _l, 0), ("cb", _l, 1)]
    JOBS_D += [("gl", _l, 0), ("gl", _l, 1), ("hb", _l, 0), ("hb", _l, 1)]
    JOBS_D += [("kc", _l, t) for t in range(NT)] + [("qc", _l, t) for t in range(NT)]
    JOBS_A += [("pk", _l)] + [("kt", _l, t) for t in range(NT)] + [("vc", _l, t) for t in range(NT)]
    JOBS_A += [("qt", _l, t) for t in range(NT)] + [("va", _l, t) for t in range(NT)]
    JOBS_D += [("ra", _l, t) for t in range(NT)]
    JOBS_A += [("kd", _l, t) for t in range(NT)]
    JOBS_D += [("att", _l, t) for t in range(NT)] + [("U", _l, c) for c in range(len(CHUNKS))]
    JOBS_D += [("oa", _l, t) for t in range(NT)]
    JOBS_S += [("s", _l, n) for n in range(NT * H)]
    JOBS_A += [("at", _l, n) for n in range(NT * H)]
    JOBS_D += [("oc", _l, t) for t in range(NT)]
    JOBS_A += [("ya", _l, t) for t in range(NT)] + [("yc", _l, t) for t in range(NT)]
    for t in range(NT):
        JOBS_A.append(("wo", _l, t))
        JOBS_D.append(("wo", _l, t))
    _norm_jobs(2 * _l + 1)
    if _l == 0:
        for _f in range(FB):
            JOBS_A.append(("g", _f))
            JOBS_D.append(("u", _f))
        JOBS_A += [("dT", _o) for _o in (0, 1, 4, 5)]
        JOBS_D += [("dT", _o) for _o in (2, 3, 6, 7)]
        for t in range(NT):
            JOBS_A.append(("dn", t))
            JOBS_D.append(("dn", t))
JOBS_D += [("lg", t) for t in range(NT)] + [("rk", t) for t in range(NT)] + [("cnt",), ("idx0",), ("idx",)]


class PsumRing:

    def __init__(self, banks, jobs, full, free):
        self.banks, self.full, self.free = banks, full, free
        self.n = {j: i for i, j in enumerate(jobs)}
        self.count = len(jobs)

    def bank(self, job):
        return self.banks[self.n[job] % len(self.banks)]

    def begin(self, pe, job):
        n = self.n[job]
        if n >= len(self.banks):
            pe.wait_ge(self.free, n - len(self.banks) + 1)
        return self.bank(job)

    def filled(self, job):
        return self.n[job] + 1

    emptied = filled


class Steps:

    def __init__(self, eng, sem):
        self.eng, self.sem, self.n = eng, sem, 0

    def __call__(self, ins):
        ins.then_inc(self.sem, 1)
        self.n += 1
        self.eng.wait_ge(self.sem, self.n)


def build(nc, A, O):
    (y_p, y_s, k_p, v_p, gla_p, conv_p, k_s, v_s, gla_s, conv_s) = O
    hx = nc.dram_tensor("normed_rows", (T, D), F32, kind="Internal").ap()
    ybuf = nc.dram_tensor("expert_rows", (MAXB * NE * P, D), F32, kind="Internal").ap()

    with ExitStack() as ctx:
        def sb(name, shape, dt=F32, stack=ctx):
            return stack.enter_context(nc.sbuf_tensor(name, shape, dt))

        def sem(name):
            return ctx.enter_context(nc.semaphore(name))

        banks = [ctx.enter_context(nc.psum_tensor(f"bank{i}", [P, 512], F32)) for i in range(8)]
        A_full, A_free = sem("A_full"), sem("A_free")
        D_full, D_free = sem("D_full"), sem("D_free")
        S_full, S_free = sem("S_full"), sem("S_free")
        RA_ = PsumRing(banks[0:3], JOBS_A, A_full, A_free)
        RD_ = PsumRing([banks[3 + (i - len(JOBS_D) + 1) % 3] for i in range(3)], JOBS_D, D_full, D_free)
        RS_ = PsumRing(banks[6:8], JOBS_S, S_full, S_free)

        x = sb("x", [P, NT, D])
        before = ExitStack()
        ring = sb("ring", [P, RING, SLOT], F32, before)
        CG = sb("CG", [P, DEPTH, 2, NT, DK], F32, before)
        SG = sb("SG", [P, DEPTH, 2, NT, DK], F32, before)
        sg = sb("sg", [P, 2, T], F32, before)
        before.close()
        raw = sb("raw", [P, PR * PIECE])
        const = sb("const_sb", [P, CONST_W])
        pcol = sb("pcol", [P, 48])
        bc = sb("bc", [P, 960])
        wga = sb("wga", [P, DEPTH, KB, GR])
        wg2 = sb("wg2", [GR, DEPTH, 2, P])
        wr = sb("wr", [P, KB, NE])
        small_ss = sb("small_ss", [P, 18 * DEPTH, 8])
        small_rs = sb("small_rs", [P, 18 * DEPTH, 8])
        half_neg = sb("half_neg", [P, 8])
        zeros = sb("zeros", [P, D // 4])
        lamt = sb("lamt", [P, 2, DEPTH])
        neglam = sb("neglam", [P, DEPTH])

        def C(name, rows=P):
            a, w = CONST[name]
            return const[0:rows, a:a + w]

        ident = C("ident")
        cc = C("cc").rearrange("p (t d) -> p t d", t=NT)
        ssn = C("ss").rearrange("p (t d) -> p t d", t=NT)

        def gcol(norm):
            at = (norm % 2) * 16 + (norm // 2) * 8
            return pcol[:, at:at + 8]

        def wconv(l, j, b):
            at = 32 + l * 6 + j * 2 + b
            return pcol[:, at:at + 1]

        def bg2(l, pair):
            return pcol[:, 44 + 2 * l + pair:45 + 2 * l + pair]

        bq = bc[:, 0:192].rearrange("p (w l d) -> p w l d", w=2, l=DEPTH)
        bl = bc[:, 192:576].rearrange("p (v l d) -> p v l d", v=4, l=DEPTH)
        bgla = bc[:, 576:768].rearrange("p (l d) -> p l d", l=DEPTH)
        bsub = bc[:, 768:960].rearrange("p (l d) -> p l d", l=DEPTH)

        front = ExitStack()
        rows_ = ExitStack()
        xhat = sb("xhat", [P, NT, D], F32, rows_)
        rows_.close()
        cut_hi = sb("cut_hi", [P, CR, CUT], FR, front)
        plain = ExitStack()
        xT = sb("xT", [P, KB, T], F32, plain)
        plain.close()
        xT_hi = sb("xT_hi", [P, KB, T], FR, front)
        up = sb("up", [P, 2, T + 4], F32, front)
        pkr = sb("pkr", [P, 8, HW], F32, front)
        pv = sb("pv", [P, DEPTH, H * DV], F32, front)
        att = sb("att", [P, NT, H, CH], F32, front)
        S = sb("S", [P, len(CHUNKS) + 1, 2, DV], F32, front)
        mix = ExitStack()

        def mb(name, shape, dt=F32):
            return sb(name, shape, dt, mix)

        over = sb("over", [P, 7552], F32, mix)
        taken = [0]

        def ov_(*shape):
            n = int(np.prod(shape))
            a = over[:, taken[0]:taken[0] + n]
            taken[0] += n
            assert taken[0] <= 7552
            names = " ".join("abc"[:len(shape)])
            return a.rearrange(f"p ({names}) -> p {names}", **dict(zip("abc", shape)))

        qT, kT = ov_(H, T), ov_(H, T)
        va, vc, sra = ov_(NT, H * DV), ov_(NT, H * DV), ov_(NT, H * DV)
        bbs, cbs = ov_(2, T), ov_(2, T)
        Yc = sra
        yb = cbs
        gla = mb("gla", [P, 9, 2, T])
        qr, kr, cum, d1, z, e1, ed, eb, qb = [gla[:, i] for i in range(9)]
        eq, ek = z, e1
        glaf = gla[:].rearrange("p i r n -> p (i r n)")
        yv = glaf[:, 2 * 2 * T:2 * 2 * T + 2 * (T + 2)].rearrange("p (b n) -> p b n", b=2)
        pe_ = glaf[:, 0:1024].rearrange("p (i c k) -> p i c k", i=2, c=2)
        am = glaf[:, 1024:1536].rearrange("p (i k) -> p i k", i=2)
        aT = glaf[:, 1536:2048].rearrange("p (i b n) -> p i b n", i=2, b=2)
        atm = glaf[:, 2048:2304]
        kdn = mb("kdn", [P, NT, 2, P])
        Ya = mb("Ya", [P, NT, H * DV])
        Yaf = Ya[:].rearrange("p t n -> p (t n)")
        brow, prow = Yaf[0:1, 0:960], Yaf[0:48, 960:960 + P]
        sq = mb("sq", [P, 2, H * DV])
        t1 = mb("t1", [P, 8 * DK])
        t2 = mb("t2", [P, 8 * DK])
        t3 = mb("t3", [P, 8 * DK])
        gaT = t2[0:GR, 0:T]
        pkT = mb("pkT", [P, H, PAST])
        mx = mb("mx", [P, 2, 2])
        nm = mb("nm", [P, 2, 2])
        sm = mb("sm", [P, 2, 2])
        rc = mb("rc", [P, 2])
        rc2 = mb("rc2", [P, 1])
        krope = xhat[:, :, 0:512].rearrange("p t (g c) -> p t g c", c=HW)
        qrope = xhat[:, :, 512:1024].rearrange("p t (g c) -> p t g c", c=HW)
        qkp = qrope
        yT = xT
        mix.close()

        ffn = ExitStack()
        xT_lo = sb("xT_lo", [P, KB, T], FR, ffn)
        hT_hi = sb("hT_hi", [P, FB, T], FR, ffn)
        hT_lo = sb("hT_lo", [P, FB, T], FR, ffn)
        prod = sb("prod", [P, T], F32, ffn)
        cut_lo = sb("cut_lo", [P, CR, CUT], FR, ffn)
        ffn.close()

        front.close()
        hmT_hi = sb("hmT_hi", [P, FEB, P], FR)
        ye = sb("ye", [P, D])
        hm = sb("hm", [P, 2, 512])
        split_hi = sb("split_hi", [P, SR, PIECE], FR)
        split_lo = sb("split_lo", [P, SR, PIECE], FR)
        lgs = sb("lgs", [P, NT, NE])
        top = sb("top", [P, NT, 8])
        topi = sb("topi", [P, NT, 8], U32)
        topf = sb("topf", [P, NT, 8])
        oh = sb("oh", [P, NT, 2, NE])
        M = sb("M", [P, NT, NE])
        rank = sb("rank", [P, NT, NE])
        rtmp = sb("rtmp", [P, NT, 2, NE])
        rk2 = sb("rk2", [P, NT, 2])
        ov = sb("ov", [P, NT, 2])
        posf = sb("posf", [P, NT, 2])
        pos = sb("pos", [P, NT, 2], U32)
        gd = sb("gd", [P, NT, 4])
        cntm = sb("cntm", [P, 4])
        npair = sb("npair", [1, 2], I32)
        rankm = sb("rankm", [P, NT, NE])
        idx = sb("idx", [P, MAXB * NE + 1], U32)
        idx0 = sb("idx0", [P, 1], U32)
        idx0f = sb("idx0f", [P, 1])
        idxf = sb("idxf", [P, MAXB * NE])
        idc = sb("idc", [P, 1], U32)
        xg = sb("xg", [P, D])
        xgT_hi = sb("xgT_hi", [P, KB, P], FR)
        xgT_lo = sb("xgT_lo", [P, KB, P], FR)
        hs = sb("hs", [P, 2, 512])
        routing = ExitStack()
        G = sb("G", [P, 2, NT, MAXB * P], BF, routing)
        tokb = sb("tokb", [P, NT, 2], BF, routing)
        routing.close()
        loop_only = ExitStack()
        hmT_lo = sb("hmT_lo", [P, FEB, P], FR, loop_only)
        loop_only.close()
        cmb = raw[:, 0:2 * NT * D].rearrange("p (n d) -> p n d", d=D)

        const_in, prow_in, brow_in, x_in, w_small = sem("const_in"), sem("prow_in"), sem("brow_in"), sem("x_in"), sem("w_small")
        wga_in, idx0_ready = sem("wga_in"), sem("idx0_ready")
        prow_zero, wg2_zero, pool_zero = sem("prow_zero"), sem("wg2_zero"), sem("pool_zero")
        past_in, hist_in, s0_in = sem("past_in"), sem("hist_in"), sem("s0_in")
        ring_full = [sem(f"ring_full{i}") for i in range(RING)]
        piece_full = [sem(f"piece_full{i}") for i in range(PR)]
        hi_ready, lo_ready, piece_used, th_ready = sem("hi_ready"), sem("lo_ready"), sem("piece_used"), sem("th_ready")
        unit_used = sem("unit_used")
        xhi_ready, cut_hi_ready, cut_lo_ready, cut_used, hT_ready = sem("xhi_ready"), sem("cut_hi_ready"), sem("cut_lo_ready"), sem("cut_used"), sem("hT_ready")
        bcast_ready, tables_ready, lam_exp = sem("bcast_ready"), sem("tables_ready"), sem("lam_exp")
        rows_sq, ss_ready, rs_ready = sem("rows_sq"), sem("ss_ready"), sem("rs_ready")
        xhat_ready = sem("xhat_ready")
        sq_ready = sem("sq_ready")
        ln_ready, d_ready, exps_ready, gk_ready = sem("ln_ready"), sem("d_ready"), sem("exps_ready"), sem("gk_ready")
        rope_ready, att_ready, state_ready, conv_ready = sem("rope_ready"), sem("att_ready"), sem("state_ready"), sem("conv_ready")
        era_ready, ya_ready, yc_ready = sem("era_ready"), sem("ya_ready"), sem("yc_ready")
        nm_ready, am_ready = sem("nm_ready"), sem("am_ready")
        k_out, v_out, st_out, cv_out, y_out = sem("k_out"), sem("v_out"), sem("st_out"), sem("cv_out"), sem("y_out")
        hx_out, gate_in, gate_out, M_ready = sem("hx_out"), sem("gate_in"), sem("gate_out"), sem("M_ready")
        G_ready, G_used, idx_ready, pairs_ready, pos_ready = sem("G_ready"), sem("G_used"), sem("idx_ready"), sem("pairs_ready"), sem("pos_ready")
        idc_ready, xg_in, ye_out, rows_out = sem("idc_ready"), sem("xg_in"), sem("ye_out"), sem("rows_out")
        g_free, u_free = sem("g_free"), sem("u_free")
        t_full, t_free, y_free = sem("t_full"), sem("t_free"), sem("y_free")
        cmb_in, cmb_used = [sem(f"cmb_in{n}") for n in range(2 * NT)], sem("cmb_used")
        pe_step, dve_step, act_step, pool_step = sem("pe_step"), sem("dve_step"), sem("act_step"), sem("pool_step")

        NS = 12

        def rs_slot(l, what, t):
            return 18 * l + {"mix": 0, "kc": 3, "qc": 6, "oa": 9, "oc": 12, "ffn": 15}[what] + t

        def ss_count(l, what, t):
            return NS * l + {"kc": 0, "qc": 3, "oa": 6, "oc": 9}[what] + t + 1

        block = ctx.enter_context(nc.Block())

        def outputs_left(eng, l):
            eng.wait_ge(v_out, 16 * 2 * (l + 1))
            eng.wait_ge(st_out, 16 * 4 * (l + 1))
            eng.wait_ge(cv_out, 16 * 4 * (l + 1))

        def wait_cut_used(eng, q):
            u, kind, which = CUTS[q]
            if kind == "g":
                eng.wait_ge(A_full, RA_.filled(("g", which)))
            elif kind == "u":
                eng.wait_ge(D_full, RD_.filled(("u", which)))
            elif which[1] == HALF - 1:
                eng.wait_ge(D_full, RD_.filled(("dT", 4 * which[0] + 3)))
            else:
                eng.wait_ge(cut_used, (HALF - 1) * which[0] + which[1] + 1)

        def raw_cut(q):
            u, kind, which = CUTS[q]
            slot = ring[:, UNIT[u] % RING, :]
            if kind == "d":
                return slot[:, CUT * (which[1] % 4):CUT * (which[1] % 4) + CUT].rearrange("p (k n) -> p k n", k=2)
            n = min(512, FF - 512 * (which // 4))
            return slot[:, 0:KB * n].rearrange("p (k n) -> p k n", k=KB)[:, :, P * (which % 4):P * (which % 4) + P]

        def split_cut(part, q):
            return part[:, q % CR, :].rearrange("p (k n) -> p k n", k=2 if CUTS[q][1] == "d" else KB)

        @block.sync
        def _(sp):
            def cols(w, a, n):
                return w[:, a:a + n].rearrange("(k p) n -> p k n", p=P)

            def source(u):
                kind = u[0]
                if kind in ("g", "u"):
                    w = A["ffn_w_gate" if kind == "g" else "ffn_w_up"]
                    n = min(512, FF - 512 * u[1])
                    return cols(w[0], 512 * u[1], n), (KB, n)
                if kind == "d":
                    n = min(8, FB - 8 * u[2])
                    return A["ffn_w_down"][0, 1024 * u[2]:1024 * u[2] + P * n, 512 * u[1]:512 * u[1] + 512].rearrange("(b p) n -> p b n", p=P), (n, 512)
                if kind == "wo":
                    return A["w_out"][u[1], 512 * u[2]:512 * u[2] + 512, :].rearrange("(b p) n -> p b n", p=P), (4, D)
                a, n = {"qk": (QA, 384), "bc": (BB, 512), "hb": (HB, 256), "kc": (KC, 384), "qc": (QC, 384),
                        "vc": (VC, 384), "va": (VA, 384), "ra": (RA, 384)}[kind]
                return cols(A["w_in"][u[1]], a, n), (KB, n)

            sp.wait_ge(const_in, 16)
            sp.wait_ge(x_in, 32)
            for l in range(DEPTH):
                sp.dma_start(wga[:, l], A["w_in"][l, :, GA:GA + GR].rearrange("(k p) n -> p k n", p=P)).then_inc(wga_in, 16)
            for n, u in enumerate(UNITS):
                src, (b, w) = source(u)
                if n >= RING:
                    if is_dense(UNITS[n - RING]):
                        sp.wait_ge(cut_lo_ready, LAST_CUT[UNITS[n - RING]] + 1)
                    else:
                        sp.wait_ge(unit_used, plain_units(n - RING + 1))
                sp.dma_start(ring[:, n % RING, 0:b * w].rearrange("p (b n) -> p b n", b=b), src).then_inc(ring_full[n % RING], 16)

            wg_v = A["moe_w_gate"][0].rearrange("e (k p) n -> e p k n", p=P)
            wu_v = A["moe_w_up"][0].rearrange("e (k p) n -> e p k n", p=P)
            wd_v = A["moe_w_down"][0].rearrange("e (c b p) n -> e c p b n", b=4, p=P)

            def pair(e, first):
                for i in range(2 * NP):
                    h, q = divmod(i, NP)
                    j, half = q // 2, q % 2
                    s = i % PR
                    sp.wait_ge(lo_ready, first + (i + 1))
                    if j < 2 * FC:
                        w = wg_v if j % 2 == 0 else wu_v
                        src = w[bass.ds(e + h, 1), :, 4 * half:4 * half + 4, 512 * (j // 2):512 * (j // 2) + 512]
                    else:
                        src = wd_v[bass.ds(e + h, 1), j - 2 * FC, :, 2 * half:2 * half + 2, :]
                    src = src.rearrange("e p k n -> p (e k) n")
                    dst = raw[:, s * PIECE:(s + 1) * PIECE].rearrange("p (k n) -> p k n", k=src.shape[1])
                    sp.dma_start(dst, src).then_inc(piece_full[s], 16)

            sp.wait_ge(unit_used, plain_units(len(UNITS)))
            sp.wait_ge(lo_ready, PR)
            with sp.Fori(0, NE // 2) as ip:
                pair(ip * 2, ip * (2 * NP))
            sp.wait_ge(pairs_ready, 1)
            more = sp.value_load(npair[0:1, 1:2], min_val=0, max_val=NE // 2 * (MAXB - 1))
            with sp.If(more > 0):
                with sp.Fori(0, more) as ip:
                    pair((ip % (NE // 2)) * 2, ip * (2 * NP) + NE * NP)

        @block.gpsimd
        def _(pool):
            step = Steps(pool, pool_step)
            nc.gpsimd.memset(half_neg[:], -0.5).then_inc(pool_zero, 1)
            nc.gpsimd.memset(prow, 0.0).then_inc(prow_zero, 1)
            pool.wait_ge(prow_zero, 1)
            pool.dma_start(prow[0:16, :], A["g_mix"].rearrange("l (k p) -> (l k) p", p=P)).then_inc(prow_in, 16)
            pool.dma_start(prow[16:32, :], A["g_ffn"].rearrange("l (k p) -> (l k) p", p=P)).then_inc(prow_in, 16)
            pool.dma_start(prow[32:44, :], A["w_conv"].rearrange("l j (b p) -> (l j b) p", p=P)).then_inc(prow_in, 16)
            pool.dma_start(prow[44:48, :].rearrange("r (h d) -> r h d", d=HW)[:, :, 0:DK],
                           A["b_g2"].rearrange("l (r h d) -> (l r) h d", r=2, h=2)).then_inc(prow_in, 16)

            def rsqrt(slot, rows, n, width):
                v, r = small_ss[0:rows, slot, 0:width], small_rs[0:rows, slot, 0:width]
                step(nc.gpsimd.tensor_scalar(v, v, 1.0 / n, EPS, ALU.mult, ALU.add))
                nc.gpsimd.tensor_tensor(r, v, half_neg[0:rows, 0:width], ALU.pow).then_inc(rs_ready, 1)
            pool.wait_ge(pool_zero, 1)
            for t, (t0, rows) in enumerate(TILES):
                pool.wait_ge(rows_sq, t + 1)
                rsqrt(rs_slot(0, "mix", t), rows, D, 1)
            step(nc.gpsimd.memset(wg2[:], 0.0))
            for l in range(DEPTH):
                for r in range(2):
                    pool.dma_start(wg2[:, l, r, :].rearrange("g (h d) -> g h d", d=HW)[:, :, 0:DK],
                                   A["w_g2"][l].rearrange("g (r h d) -> g r h d", r=2, h=2)[:, r]).then_inc(w_small, 16)
            pool.dma_start(wr[:], A["w_router"][0].rearrange("(k p) n -> p k n", p=P)).then_inc(w_small, 16)
            for tile in (att[:], S[:], up[:], pkr[:], zeros[:]):
                nc.gpsimd.memset(tile, 0.0).then_inc(pool_zero, 1)
            pool.wait_ge(pool_zero, 6)

            def loads(l):
                pool.dma_start(pkr[:, :, 0:DK], A["cache_k"][l, 0].rearrange("t h c d -> t (h c) d")).then_inc(past_in, 16)
                pool.dma_start(pv[:, l, :], A["cache_v"][l, 0].rearrange("t h d -> t (h d)")).then_inc(past_in, 16)
                for h in range(2):
                    pool.dma_start(S[HW * h:HW * h + DK, 5], A["state_gla"][l, 0].rearrange("(r h) d e -> h d r e", h=2)[h]).then_inc(s0_in, 16)
                for b in range(2):
                    with nc.allow_non_contiguous_dma(reason="two columns of history"):
                        pool.dma_start(up[:, b, SEQ + 2:SEQ + 4], A["state_conv"][l, 0, :, b * P:b * P + P].rearrange("j p -> p j")).then_inc(hist_in, 16)

            loads(0)

            pool.wait_ge(const_in, 16)
            pool.wait_ge(bcast_ready, 1)
            hd = DK // 2
            for l in range(DEPTH):
                for w in range(2):
                    g = bq[:, w, l, :]
                    nc.gpsimd.tensor_tensor(CG[:, l, w], cc, g.unsqueeze(1).to_broadcast([P, NT, DK]), ALU.mult)
                    nc.gpsimd.tensor_tensor(SG[:, l, w, :, 0:hd], ssn[:, :, 0:hd], g[:, hd:DK].unsqueeze(1).to_broadcast([P, NT, hd]), ALU.mult)
                    nc.gpsimd.tensor_tensor(SG[:, l, w, :, hd:DK], ssn[:, :, hd:DK], g[:, 0:hd].unsqueeze(1).to_broadcast([P, NT, hd]), ALU.mult)
                last = nc.gpsimd.tensor_scalar(bsub[:, l], bsub[:, l], 1.0 - LAM0[l], None, ALU.mult)
                last.then_inc(tables_ready, 1)

            def keys_and_history_out(l):
                for t in range(NT):
                    pool.wait_ge(rope_ready, 6 * l + t + 1)
                    dst = (k_p[l, 0, P * t:P * t + P] if t < 2 else k_s[l, 0]).rearrange("t h c d -> t (h c) d")
                    pool.dma_start(dst, krope[0:TILES[t][1], t, :, 0:DK]).then_inc(k_out, 16)
                pool.wait_ge(D_free, RD_.emptied(("hb", l, 1)))
                for dst, a in ((conv_p, SEQ), (conv_s, T + 2)):
                    for b in range(2):
                        with nc.allow_non_contiguous_dma(reason="two columns of history"):
                            pool.dma_start(dst[l, 0, :, b * P:b * P + P].rearrange("j p -> p j"), up[:, b, a:a + 2]).then_inc(cv_out, 16)

            def states_out(l):
                pool.wait_ge(D_free, RD_.emptied(("U", l, 4)))
                for dst, c in ((gla_p, 3), (gla_s, 4)):
                    for h in range(2):
                        pool.dma_start(dst[l, 0].rearrange("(r h) d e -> h d r e", h=2)[h], S[HW * h:HW * h + DK, c]).then_inc(st_out, 16)

            for l in range(DEPTH):
                if l:
                    for t, (t0, rows) in enumerate(TILES):
                        pool.wait_ge(rows_sq, 6 * l + t + 1)
                        rsqrt(rs_slot(l, "mix", t), rows, D, 1)
                    pool.wait_ge(A_free, RA_.emptied(("pk", 0)))
                    pool.wait_ge(st_out, 16 * 4)
                    pool.wait_ge(cv_out, 16 * 4)
                    loads(l)
                for what, n, width in (("kc", DK, 8), ("qc", DK, 8), ("oa", DV, 4), ("oc", DV, 4)):
                    for t, (t0, rows) in enumerate(TILES):
                        pool.wait_ge(ss_ready, ss_count(l, what, t))
                        rsqrt(rs_slot(l, what, t), rows, n, width)
                    if what == "kc":
                        keys_and_history_out(l)
                    if what == "oa":
                        states_out(l)
                for t, (t0, rows) in enumerate(TILES):
                    pool.wait_ge(rows_sq, 6 * l + 3 + t + 1)
                    rsqrt(rs_slot(l, "ffn", t), rows, D, 1)

            for t, (t0, rows) in enumerate(TILES):
                pool.wait_ge(xhat_ready, 9 + t + 1)
                pool.dma_start(hx[t0:t0 + rows, :], xhat[0:rows, t, :]).then_inc(hx_out, 16)
            pool.wait_ge(hx_out, 16 * NT)
            pool.wait_ge(pairs_ready, 1)
            pairs = pool.value_load(npair[0:1, 0:1], min_val=NE // 2, max_val=NE // 2 * MAXB)

            def gather():
                pool.indirect_dma_start(out=xg[:], out_offset=None, in_=hx[:, :],
                                        in_offset=bass.IndirectOffsetOnAxis(ap=idc[:, 0:1], axis=0)).then_inc(xg_in, 16)

            pool.wait_ge(idx0_ready, 1)
            nc.gpsimd.tensor_copy(idc[:, 0:1], idx0[:]).then_inc(idc_ready, 1)
            pool.wait_ge(idc_ready, 1)
            with pool.Fori(0, pairs * 2) as n:
                gather()
                pool.wait_ge(idx_ready, 1)
                pool.wait_ge(t_full, n * 9 + 2)
                pool.wait_ge(xg_in, n * 16 + 16)
                nc.gpsimd.tensor_copy(idc[:, 0:1], idx[:, bass.ds(n + 1, 1)]).then_inc(idc_ready, 1)
                pool.wait_ge(idc_ready, n + 2)
            gather()
            pool.wait_ge(pos_ready, 1)
            pool.wait_ge(rows_out, 1)
            for t, (t0, rows) in enumerate(TILES):
                for k in range(2):
                    pool.indirect_dma_start(out=cmb[0:rows, 2 * t + k, :], out_offset=None, in_=ybuf[:, :],
                                            in_offset=bass.IndirectOffsetOnAxis(ap=pos[0:rows, t, k:k + 1], axis=0)).then_inc(cmb_in[2 * t + k], 16)

        @block.scalar
        def _(act):
            step = Steps(act, act_step)
            hs_n = [0]
            act.dma_start(const[:], A["const"]).then_inc(const_in, 16)
            act.dma_start(x[:, 0:2, :], A["x_prompt"][0].rearrange("(t p) d -> p t d", p=P)).then_inc(x_in, 16)
            act.dma_start(x[0:DEC, 2, :], A["x_sample"][0]).then_inc(x_in, 16)
            at = 0
            for name in ("g_q", "g_k", "lambda_q1", "lambda_k1", "lambda_q2", "lambda_k2", "g_gla", "g_sub"):
                n = DEPTH * A[name].shape[1]
                act.dma_start(brow[0:1, at:at + n], A[name].rearrange("l d -> (l d)").unsqueeze(0)).then_inc(brow_in, 16)
                at += n

            def norm_squares(i):
                for t, (t0, rows) in enumerate(TILES):
                    if i == 0:
                        act.wait_ge(x_in, 32)
                    else:
                        job = ("wo", i // 2, t) if i % 2 else ("dn", t)
                        act.wait_ge(A_free, RA_.emptied(job))
                        act.wait_ge(D_free, RD_.emptied(job))
                        if i % 2:
                            act.wait_ge(k_out, 16 * 3 * (i // 2 + 1))
                    nc.scalar.activation(xhat[0:rows, t, :], x[0:rows, t, :], ACT.Square,
                                         accum_out=small_ss[0:rows, rs_slot(i // 2, "ffn" if i % 2 else "mix", t), 0:1]).then_inc(rows_sq, 1)

            def norm_split(i):
                for t, (t0, rows) in enumerate(TILES):
                    for full, R, k0 in ((A_full, RA_, 0), (D_full, RD_, 4)):
                        act.wait_ge(full, R.filled(("xt", i, t)))
                        b = R.bank(("xt", i, t)).rearrange("p (k n) -> p k n", k=4)
                        for k in range(4):
                            last = nc.scalar.activation(xT_hi[:, k0 + k, t0:t0 + rows], b[:, k, 0:rows], ACT.Copy, scale=gcol(i)[:, k0 + k:k0 + k + 1])
                        last.then_inc(xhi_ready, 1)

            def norm_evacuate(i):
                for t, (t0, rows) in enumerate(TILES):
                    act.wait_ge(A_full, RA_.filled(("xt", i, t)))
                    b = RA_.bank(("xt", i, t)).rearrange("p (k n) -> p k n", k=4)
                    for k in range(4):
                        last = nc.scalar.activation(xT[:, k, t0:t0 + rows], b[:, k, 0:rows], ACT.Copy, scale=gcol(i)[:, k:k + 1])
                    last.then_inc(A_free, 1)

            norm_squares(0)
            act.wait_ge(A_full, RA_.filled(("par",)))
            nc.scalar.copy(pcol[:], RA_.bank(("par",))[:, 0:48]).then_inc(A_free, 1)
            act.wait_ge(A_full, RA_.filled(("bcast", 0)))
            nc.scalar.copy(bc[:, 0:480], RA_.bank(("bcast", 0))[:, 0:480]).then_inc(A_free, 1)
            act.wait_ge(A_free, 1)
            act.wait_ge(lam_exp, 1)
            nc.scalar.activation(lamt[:], lamt[:], ACT.Exp).then_inc(lam_exp, 1)

            for l in range(DEPTH):
                if l:
                    norm_squares(2 * l)
                norm_evacuate(2 * l)

                def copy_a(job, out, in_):
                    act.wait_ge(A_full, RA_.filled(job))
                    nc.scalar.copy(out, in_).then_inc(A_free, 1)

                copy_a(("ga", l), gaT, RA_.bank(("ga", l))[0:GR, 0:T])
                for t, (t0, rows) in enumerate(TILES):
                    copy_a(("qk", l, t), qkp[0:rows, t, :, 0:DK], RA_.bank(("qk", l, t))[0:rows, 0:384].rearrange("p (g d) -> p g d", g=8))
                for t, (t0, rows) in enumerate(TILES):
                    act.wait_ge(A_full, RA_.filled(("qkt", l, t)))
                    b = RA_.bank(("qkt", l, t)).rearrange("p (r n) -> p r n", r=4)
                    nc.scalar.copy(qr[:, :, t0:t0 + rows], b[:, 0:2, 0:rows])
                    nc.scalar.copy(kr[:, :, t0:t0 + rows], b[:, 2:4, 0:rows]).then_inc(A_free, 1)
                for b in range(2):
                    copy_a(("bb", l, b), bbs[:, b], RA_.bank(("bb", l, b))[:, 0:T])
                for b in range(2):
                    copy_a(("cb", l, b), cbs[:, b], RA_.bank(("cb", l, b))[:, 0:T])
                act.wait_ge(D_free, RD_.emptied(("gl", l, 1)))
                step(nc.scalar.activation(e1, z, ACT.Abs))
                step(nc.scalar.activation(e1, e1, ACT.Exp, scale=-1.0))
                nc.scalar.activation(e1, e1, ACT.Ln, bias=1.0).then_inc(ln_ready, 1)

                def squares(src, what, t, rows):
                    n = hs_n[0]
                    hs_n[0] += 1
                    if n >= 2:
                        act.wait_ge(ss_ready, n - 1)
                    nc.scalar.activation(sq[0:rows, n % 2, :], src, ACT.Square).then_inc(sq_ready, 1)

                def squares_of(what):
                    for t, (t0, rows) in enumerate(TILES):
                        act.wait_ge(D_full, RD_.filled((what, l, t)))
                        squares(RD_.bank((what, l, t))[0:rows, 0:384], what, t, rows)

                squares_of("kc")
                act.wait_ge(d_ready, 2 * l + 2)
                nc.scalar.activation(eq, d1, ACT.Exp, scale=1.0 / 16)
                nc.scalar.activation(ek, d1, ACT.Exp, scale=-1.0 / 16)
                nc.scalar.activation(eb, cum, ACT.Exp, scale=1.0 / 16)
                nc.scalar.activation(ed, ed, ACT.Exp, scale=1.0 / 16).then_inc(exps_ready, 1)
                squares_of("qc")
                copy_a(("pk", l), pkT[:], RA_.bank(("pk", l)).rearrange("p (h n) -> p h n", h=H))
                for t, (t0, rows) in enumerate(TILES):
                    copy_a(("kt", l, t), kT[:, :, t0:t0 + rows], RA_.bank(("kt", l, t)).rearrange("p (h n) -> p h n", h=H)[:, :, 0:rows])
                for t, (t0, rows) in enumerate(TILES):
                    if l and t == 0:
                        act.wait_ge(v_out, 16 * 2)
                    copy_a(("vc", l, t), vc[0:rows, t], RA_.bank(("vc", l, t))[0:rows, 0:384])
                for t, (t0, rows) in enumerate(TILES):
                    copy_a(("qt", l, t), qT[:, :, t0:t0 + rows], RA_.bank(("qt", l, t)).rearrange("p (h n) -> p h n", h=H)[:, :, 0:rows])
                for t, (t0, rows) in enumerate(TILES):
                    copy_a(("va", l, t), va[0:rows, t], RA_.bank(("va", l, t))[0:rows, 0:384])
                act.wait_ge(A_free, RA_.emptied(("vc", l, 2)))
                act.dma_start(v_p[l, 0].rearrange("(t p) h d -> p t (h d)", p=P), vc[:, 0:2]).then_inc(v_out, 16)
                act.dma_start(v_s[l, 0].rearrange("t h d -> t (h d)"), vc[0:DEC, 2]).then_inc(v_out, 16)
                for t, (t0, rows) in enumerate(TILES):
                    act.wait_ge(D_full, RD_.filled(("ra", l, t)))
                    nc.scalar.activation(sra[0:rows, t], RD_.bank(("ra", l, t))[0:rows, 0:384], ACT.Exp, scale=-1.0).then_inc(era_ready, 1)
                for t, (t0, rows) in enumerate(TILES):
                    copy_a(("kd", l, t), kdn[0:rows, t], RA_.bank(("kd", l, t)).rearrange("p (r n) -> p r n", r=2)[0:rows, :, 0:P])
                squares_of("oa")
                for n in range(NT * H + 3):
                    if n < NT * H:
                        t = n // H
                        rows, keys = TILES[t][1], [128, 256, 192][t]
                        act.wait_ge(nm_ready, NT * H * l + n + 1)
                        if n >= 2:
                            act.wait_ge(am_ready, NT * H * l + n - 1)
                        s = RS_.bank(("s", l, n)).rearrange("p (c k) -> p c k", c=2)
                        for c in range(2):
                            last = nc.scalar.activation(pe_[0:rows, n % 2, c, 0:keys], s[0:rows, c, 0:keys], ACT.Exp,
                                                        bias=nm[0:rows, n % 2, c:c + 1], scale=SC, accum_out=sm[0:rows, n % 2, c:c + 1])
                        last.then_inc(S_free, 1)
                    if 2 <= n <= NT * H + 1:
                        m = n - 2
                        t = m // H
                        rows = TILES[t][1]
                        act.wait_ge(A_full, RA_.filled(("at", l, m)))
                        b = RA_.bank(("at", l, m)).rearrange("p (k n) -> p k n", k=4)
                        if t < 2:
                            nc.scalar.copy(aT[:, m % 2, 0:t + 1, :], b[:, 0:t + 1, :]).then_inc(A_free, 1)
                        else:
                            nc.scalar.copy(aT[:, m % 2, 0, 0:rows], b[:, 0, 0:rows])
                            nc.scalar.copy(aT[0:DEC, m % 2, 1, 0:rows], b[0:DEC, 1, 0:rows]).then_inc(A_free, 1)
                    if n in (H + 2, 2 * H + 2, 3 * H + 2):
                        t = n // H - 1
                        rows = TILES[t][1]
                        act.wait_ge(D_full, RD_.filled(("oc", l, t)))
                        squares(RD_.bank(("oc", l, t))[0:rows, 0:384], "oc", t, rows)
                for what, b0 in (("ya", 0), ("yc", 5)):
                    for t, (t0, rows) in enumerate(TILES):
                        copy_a((what, l, t), yT[:, b0:b0 + 3, t0:t0 + rows], RA_.bank((what, l, t)).rearrange("p (k n) -> p k n", k=4)[:, 0:3, 0:rows])

                norm_squares(2 * l + 1)
                outputs_left(act, l)
                if l:
                    norm_evacuate(2 * l + 1)
                else:
                    norm_split(1)
                    act.wait_ge(pool_zero, 6)
                    act.dma_start(ybuf[NE * P:, :].rearrange("(p n) (c d) -> p (n c) d", p=P, c=4),
                                  zeros[:].unsqueeze(1).to_broadcast([P, (MAXB - 1) * NE * 4, D // 4])).then_inc(ye_out, 16)
                    act.wait_ge(D_full, RD_.filled(("xt", 1, 2)))
                    for q in range(len(CUTS) + 3):
                        if q >= CR:
                            wait_cut_used(act, q - CR)
                        if q in (DOWN0 + HALF + 2, len(CUTS) + 2):
                            for job, o in DOWN_BANKS[q == len(CUTS) + 2]:
                                if job == "A":
                                    copy_a(("dT", o), xT[:, o, :], RA_.bank(("dT", o))[:, 0:T])
                        if q < len(CUTS):
                            if q == 0 or CUTS[q][0] not in [c[0] for c in CUTS[:q]]:
                                n = UNIT[CUTS[q][0]]
                                act.wait_ge(ring_full[n % RING], 16 * (n // RING + 1))
                            nc.scalar.copy(split_cut(cut_hi, q), raw_cut(q)).then_inc(cut_hi_ready, 1)
                        if q % 2 and CR <= q < DOWN0 + CR:
                            f = (q - CR) // 2
                            if f >= 2:
                                act.wait_ge(D_free, RD_.emptied(("u", f - 2)))
                            act.wait_ge(A_full, RA_.filled(("g", f)))
                            nc.scalar.activation(sg[:, f % 2], RA_.bank(("g", f))[:, 0:T], ACT.Silu).then_inc(A_free, 1)

            act.wait_ge(gate_in, 1)
            nc.scalar.activation(gd[:, :, 1:2], gd[:, :, 0:1], ACT.Exp).then_inc(gate_out, 1)

            act.nop().then_inc(g_free, 1)
            act.nop().then_inc(y_free, 1)
            act.wait_ge(pairs_ready, 1)
            pairs = act.value_load(npair[0:1, 0:1], min_val=NE // 2, max_val=NE // 2 * MAXB)
            tb = [banks[4], banks[5]]

            def xg_hi(base, first):
                for k in range(KB):
                    if k % 4 == 0:
                        act.wait_ge(t_full, base + k // 4 + 1)
                    b = tb[(first + k // 4) % 2]
                    last = nc.scalar.activation(xgT_hi[:, k, :], b[:, 128 * (k % 4):128 * (k % 4) + 128], ACT.Copy, scale=gcol(3)[:, k:k + 1])
                    if k % 4 == 3:
                        last.then_inc(th_ready, 1)

            def piece_hi(i):
                return nc.scalar.copy(split_hi[:, i % SR, :], raw[:, (i % PR) * PIECE:(i % PR + 1) * PIECE]).then_inc(hi_ready, 1)

            for i in range(SR):
                act.wait_ge(piece_full[i], 16)
                piece_hi(i)
            xg_hi(0, 0)
            with act.Fori(0, pairs) as ip:
                with act.If(ip > 0):
                    for i in range(SR):
                        act.wait_ge(piece_full[i], ip * (16 * 2 * NP // PR) + 16)
                        act.wait_ge(piece_used, ip * (2 * NP) + (i + 1))
                        piece_hi(i)
                for i in range(2 * NP):
                    h, q = divmod(i, NP)
                    if i >= SR:
                        act.wait_ge(piece_full[i % PR], ip * (16 * 2 * NP // PR) + 16 * (i // PR + 1))
                        act.wait_ge(piece_used, ip * (2 * NP) + (i + 1))
                        piece_hi(i)
                    if q % 4 == 0 and 1 <= q // 4 <= FC:
                        j = q // 4 - 1
                        m = FC * h + j
                        act.wait_ge(piece_used, ip * (2 * NP) + (NP * h + 4 * j + 2 + SR))
                        act.wait_ge(u_free, ip * (2 * FC) + max(m, 1))
                        nc.scalar.activation(hs[:, m % 2, :], banks[m % 2][:], ACT.Silu).then_inc(g_free, 1)
                    if q in HT_AT:
                        j = HT_AT.index(q)
                        n = 2 + 9 * h + j
                        act.wait_ge(t_full, ip * 18 + (n + 1))
                        nc.scalar.copy(hmT_hi[:, 4 * j:4 * j + 4, :].rearrange("p b n -> p (b n)"), tb[n % 2][:]).then_inc(th_ready, 1)
                    if q == X_AT:
                        xg_hi(ip * 18 + (9 * h + 9), 9 * h + 9)
                    if q == NP - 1:
                        act.wait_ge(piece_used, ip * (2 * NP) + (NP * (h + 1) + SR))
                        act.wait_ge(ye_out, ip * 32 + 16 * (h + 1))
                        nc.scalar.copy(ye[:, 0:512], banks[6][:])
                        nc.scalar.copy(ye[:, 512:1024], banks[7][:]).then_inc(y_free, 1)
                        act.wait_ge(y_free, ip * 2 + (h + 2))
                        act.dma_start(ybuf[bass.ds(ip * (2 * P) + h * P, P), :], ye[:]).then_inc(ye_out, 16)
            act.wait_ge(ye_out, pairs * 32 + 16)
            nc.scalar.copy(hs[0:1, 0, 0:1], ye[0:1, 0:1]).then_inc(rows_out, 1)
            for t in range(NT):
                act.wait_ge(cmb_used, 2 * (t + 1))
                act.dma_start(y_p[0, P * t:P * t + P] if t < 2 else y_s[0], x[0:TILES[t][1], t, :]).then_inc(y_out, 16)
            act.wait_ge(y_out, 16 * NT)
            act.wait_ge(k_out, 16 * NT * DEPTH)
            act.wait_ge(v_out, 16 * 2 * DEPTH)
            act.wait_ge(st_out, 16 * 4 * DEPTH)
            act.wait_ge(cv_out, 16 * 4 * DEPTH)
            act.wait_ge(hx_out, 16 * NT)

        @block.vector
        def _(dve):
            step = Steps(dve, dve_step)
            V = nc.vector
            dve.wait_ge(D_full, RD_.filled(("bcast", 1)))
            V.tensor_copy(bc[:, 480:960], RD_.bank(("bcast", 1))[:, 0:480]).then_inc(D_free, 1)
            dve.wait_ge(A_free, RA_.emptied(("bcast", 0)))
            dve.wait_ge(D_free, RD_.emptied(("bcast", 1)))
            V.memset(neglam[:], 0.0).then_inc(bcast_ready, 1)
            lp = t1[:, 0:4 * DK].rearrange("p (v l d) -> p v l d", v=2, l=DEPTH)
            step(V.tensor_tensor(lp[:, 0], bl[:, 0], bl[:, 1], ALU.mult))
            step(V.tensor_tensor(lp[:, 1], bl[:, 2], bl[:, 3], ALU.mult))
            V.tensor_reduce(lamt[:], lp, AX_X, ALU.add).then_inc(lam_exp, 1)
            dve.wait_ge(lam_exp, 2)
            step(V.tensor_tensor(neglam[:], lamt[:, 1], lamt[:, 0], ALU.subtract))
            for l in range(DEPTH):
                step(V.tensor_scalar(neglam[:, l:l + 1], neglam[:, l:l + 1], -LAM0[l], None, ALU.add))

            def norm(i):
                for t, (t0, rows) in enumerate(TILES):
                    s = rs_slot(i // 2, "ffn" if i % 2 else "mix", t)
                    dve.wait_ge(rs_ready, s + 1)
                    V.tensor_scalar(xhat[0:rows, t, :], x[0:rows, t, :], small_rs[0:rows, s, 0:1], None, ALU.mult).then_inc(xhat_ready, 1)
                for t, (t0, rows) in enumerate(TILES):
                    job = ("xt", i, t)
                    dve.wait_ge(D_full, RD_.filled(job))
                    if i == 0 and t == 0:
                        dve.wait_ge(A_free, RA_.emptied(("par",)))
                    V.tensor_tensor(xT[:, 4:8, t0:t0 + rows], RD_.bank(job).rearrange("p (k n) -> p k n", k=4)[:, :, 0:rows],
                                    gcol(i)[:, 4:8].unsqueeze(2).to_broadcast([P, 4, rows]), ALU.mult).then_inc(D_free, 1)

            def norm_split(i):
                for t, (t0, rows) in enumerate(TILES):
                    s = rs_slot(i // 2, "ffn", t)
                    dve.wait_ge(rs_ready, s + 1)
                    V.tensor_scalar(xhat[0:rows, t, :], x[0:rows, t, :], small_rs[0:rows, s, 0:1], None, ALU.mult).then_inc(xhat_ready, 1)
                for t, (t0, rows) in enumerate(TILES):
                    job = ("xt", i, t)
                    for n, (full, free, R, k0) in enumerate(((A_full, A_free, RA_, 0), (D_full, D_free, RD_, 4))):
                        dve.wait_ge(full, R.filled(job))
                        dve.wait_ge(xhi_ready, 2 * t + n + 1)
                        b = R.bank(job).rearrange("p (k n) -> p k n", k=4)
                        for k in range(4):
                            last = V.scalar_tensor_tensor(out=xT_lo[:, k0 + k, t0:t0 + rows], in0=b[:, k, 0:rows], scalar=gcol(i)[:, k0 + k:k0 + k + 1],
                                                          in1=xT_hi[:, k0 + k, t0:t0 + rows].bitcast(F32), op0=ALU.mult, op1=ALU.subtract)
                        last.then_inc(free, 1)

            def sum_squares(l, what, t, rows, groups):
                n = ss_count(l, what, t)
                dve.wait_ge(sq_ready, n)
                V.tensor_reduce(small_ss[0:rows, rs_slot(l, what, t), 0:groups],
                                sq[0:rows, (n - 1) % 2, :].rearrange("p (g d) -> p g d", g=groups), AX_X, ALU.add).then_inc(ss_ready, 1)

            def scaled(l, what, t, rows, groups, out):
                s = rs_slot(l, what, t)
                dve.wait_ge(rs_ready, s + 1)
                V.tensor_tensor(out[0:rows].rearrange("p (g d) -> p g d", g=groups),
                                RD_.bank((what, l, t))[0:rows, 0:384].rearrange("p (g d) -> p g d", g=groups),
                                small_rs[0:rows, s, 0:groups].unsqueeze(2).to_broadcast([rows, groups, 384 // groups]),
                                ALU.mult).then_inc(D_free, 1)
                dve.wait_ge(D_free, RD_.emptied((what, l, t)))

            for l in range(DEPTH):
                norm(2 * l)
                for r in range(2):
                    dve.wait_ge(D_full, RD_.filled(("gl", l, r)))
                    V.tensor_scalar(z[:, r], RD_.bank(("gl", l, r))[:, 0:T], bg2(l, r), None, ALU.add).then_inc(D_free, 1)
                    dve.wait_ge(D_free, RD_.emptied(("gl", l, r)))
                step(V.tensor_scalar(cum, z, 0.0, None, ALU.min))
                for b in range(2):
                    dve.wait_ge(D_full, RD_.filled(("hb", l, b)))
                    dve.wait_ge(A_free, RA_.emptied(("cb", l, b)))
                    if b == 0:
                        dve.wait_ge(pool_zero, 6)
                        dve.wait_ge(hist_in, 32 * (l + 1))
                    hbk = RD_.bank(("hb", l, b))
                    step(V.tensor_tensor(up[:, b, 2:2 + SEQ], hbk[:, 0:SEQ], cbs[:, b, 0:SEQ], ALU.mult))
                    V.tensor_tensor(up[:, b, SEQ + 4:T + 4], hbk[:, SEQ:T], cbs[:, b, SEQ:T], ALU.mult).then_inc(D_free, 1)
                dve.wait_ge(D_free, RD_.emptied(("hb", l, 1)))
                dve.wait_ge(ln_ready, l + 1)
                step(V.tensor_tensor(d1, cum, e1, ALU.subtract))
                for r in range(2):
                    step(V.tensor_tensor_scan(cum[:, r], C("scan"), d1[:, r], 0.0, ALU.mult, ALU.add))
                c5 = cum.rearrange("p r (c n) -> p (r c) n", n=CH)
                V.tensor_tensor(d1.rearrange("p r (c n) -> p (r c) n", n=CH), c5,
                                c5[:, :, CH // 2 - 1:CH // 2].to_broadcast([P, 10, CH]), ALU.subtract).then_inc(d_ready, 1)
                V.tensor_tensor(ed.rearrange("p r (c n) -> p (r c) n", n=CH),
                                c5[:, :, CH - 1:CH].to_broadcast([P, 10, CH]), c5, ALU.subtract).then_inc(d_ready, 1)

                def rope(what, out):
                    w = {"qc": 0, "kc": 1}[what]
                    hd = DK // 2
                    for t, (t0, rows) in enumerate(TILES):
                        sum_squares(l, what, t, rows, 8)
                    if what == "kc":
                        dve.wait_ge(tables_ready, l + 1)
                    for t, (t0, rows) in enumerate(TILES):
                        scaled(l, what, t, rows, 8, t1)
                        v = t1[0:rows].rearrange("p (g d) -> p g d", g=8)
                        a = t2[0:rows].rearrange("p (g d) -> p g d", g=8)
                        b = t3[0:rows].rearrange("p (g d) -> p g d", g=8)

                        def tab(x_, lo, hi):
                            return x_[0:rows, l, w, t, lo:hi].unsqueeze(1).to_broadcast([rows, 8, hi - lo])

                        V.tensor_tensor(a, v, tab(CG, 0, DK), ALU.mult)
                        V.tensor_tensor(b[:, :, 0:hd], v[:, :, hd:DK], tab(SG, 0, hd), ALU.mult)
                        step(V.tensor_tensor(b[:, :, hd:DK], v[:, :, 0:hd], tab(SG, hd, DK), ALU.mult))
                        V.tensor_tensor(out[0:rows, t, :, 0:DK], a, b, ALU.add).then_inc(rope_ready, 1)
                        dve.wait_ge(rope_ready, 6 * l + (0 if what == "kc" else 3) + t + 1)

                rope("kc", krope)
                dve.wait_ge(exps_ready, l + 1)
                dve.wait_ge(A_free, RA_.emptied(("qkt", l, 2)))
                V.tensor_tensor(ed, ed, kr, ALU.mult).then_inc(gk_ready, 1)
                qs = dict(scalar=SC, op0=ALU.mult, op1=ALU.mult)
                fl = lambda a: a.rearrange("p r n -> p (r n)")
                V.scalar_tensor_tensor(out=fl(qb), in0=fl(qr), in1=fl(eb), **qs)
                V.scalar_tensor_tensor(out=fl(eq), in0=fl(qr), in1=fl(eq), **qs)
                V.tensor_tensor(ek, ek, kr, ALU.mult).then_inc(gk_ready, 1)
                rope("qc", qrope)
                for b in range(2):
                    step(V.tensor_scalar(yv[:, b], up[:, b, 0:T + 2], wconv(l, 0, b), None, ALU.mult))
                    for j in (1, 2):
                        step(V.scalar_tensor_tensor(out=yv[:, b], in0=up[:, b, j:j + T + 2], scalar=wconv(l, j, b), in1=yv[:, b],
                                                    op0=ALU.mult, op1=ALU.add))
                V.tensor_tensor(yb[:, :, 0:SEQ], yv[:, :, 0:SEQ], bbs[:, :, 0:SEQ], ALU.mult)
                V.tensor_tensor(yb[:, :, SEQ:T], yv[:, :, SEQ + 2:T + 2], bbs[:, :, SEQ:T], ALU.mult).then_inc(conv_ready, 1)
                for t, (t0, rows) in enumerate(TILES):
                    dve.wait_ge(era_ready, NT * l + t + 1)
                    s = sra[0:rows, t]
                    step(V.tensor_scalar(s, s, 1.0, None, ALU.add))
                    step(V.reciprocal(s, s))
                    V.tensor_tensor(s, RD_.bank(("ra", l, t))[0:rows, 0:384], s, ALU.mult).then_inc(D_free, 1)
                msk = C("attm").bitcast(I32)
                for t, (t0, rows) in enumerate(TILES):
                    dve.wait_ge(D_full, RD_.filled(("att", l, t)))
                    V.copy_predicated(att[0:rows, t].rearrange("p h n -> p (h n)"), msk[0:rows], RD_.bank(("att", l, t))[0:rows, 0:H * CH]).then_inc(D_free, 1)
                ebc = eb.rearrange("p r (c n) -> p r c n", n=CH)
                for c in range(len(CHUNKS)):
                    dve.wait_ge(D_full, RD_.filled(("U", l, c)))
                    U = RD_.bank(("U", l, c))[:, 0:2 * DV].rearrange("p (r d) -> p r d", r=2)
                    if c == 0:
                        if l:
                            dve.wait_ge(st_out, 16 * 4)
                        V.tensor_copy(S[:, 0], U).then_inc(D_free, 1)
                    else:
                        prev = 5 if c == 4 else c - 1
                        if c == 4:
                            dve.wait_ge(s0_in, 32 * (l + 1))
                        step(V.scalar_tensor_tensor(out=S[:, c, 0], in0=S[:, prev, 0], scalar=ebc[:, 0, c, CH - 1:CH], in1=U[:, 0],
                                                    op0=ALU.mult, op1=ALU.add))
                        V.scalar_tensor_tensor(out=S[:, c, 1], in0=S[:, prev, 1], scalar=ebc[:, 1, c, CH - 1:CH], in1=U[:, 1],
                                               op0=ALU.mult, op1=ALU.add).then_inc(D_free, 1)
                    dve.wait_ge(D_free, RD_.emptied(("U", l, c)))

                def head_norm(what, t, rows, gain):
                    scaled(l, what, t, rows, H, t1)
                    return (t1[0:rows].rearrange("p (g d) -> p g d", g=H),
                            gain[0:rows, l].unsqueeze(1).to_broadcast([rows, H, DV]))

                for n in range(NT * H + 5):
                    if n < NT * H:
                        t = n // H
                        rows, keys = TILES[t][1], [128, 256, 192][t]
                        dve.wait_ge(S_full, RS_.filled(("s", l, n)))
                        step(V.tensor_reduce(mx[0:rows, n % 2], RS_.bank(("s", l, n)).rearrange("p (c k) -> p c k", c=2)[0:rows, :, 0:keys], AX_X, ALU.max))
                        V.tensor_scalar(nm[0:rows, n % 2], mx[0:rows, n % 2], -SC, None, ALU.mult).then_inc(nm_ready, 1)
                    if 1 <= n <= NT * H:
                        m = n - 1
                        t = m // H
                        rows, keys = TILES[t][1], [128, 256, 192][t]
                        dve.wait_ge(S_free, RS_.emptied(("s", l, m)))
                        step(V.reciprocal(rc[0:rows], sm[0:rows, m % 2]))
                        step(V.tensor_tensor(rc2[0:rows], rc[0:rows, 1:2], neglam[0:rows, l:l + 1], ALU.mult))
                        if m >= 2:
                            dve.wait_ge(A_full, RA_.filled(("at", l, m - 2)))
                        step(V.tensor_scalar(atm[0:rows, 0:keys], pe_[0:rows, m % 2, 1, 0:keys], rc2[0:rows], None, ALU.mult))
                        V.scalar_tensor_tensor(out=am[0:rows, m % 2, 0:keys], in0=pe_[0:rows, m % 2, 0, 0:keys], scalar=rc[0:rows, 0:1],
                                               in1=atm[0:rows, 0:keys], op0=ALU.mult, op1=ALU.add).then_inc(am_ready, 1)
                        dve.wait_ge(am_ready, NT * H * l + m + 1)
                    if n == 0:
                        for t, (t0, rows) in enumerate(TILES):
                            sum_squares(l, "oa", t, rows, H)
                    if 1 <= n <= NT:
                        t, rows = n - 1, TILES[n - 1][1]
                        v, g = head_norm("oa", t, rows, bgla)
                        step(V.tensor_tensor(t2[0:rows].rearrange("p (g d) -> p g d", g=H), v, g, ALU.mult))
                        V.tensor_tensor(Ya[0:rows, t], t2[0:rows], sra[0:rows, t], ALU.mult).then_inc(ya_ready, 1)
                        dve.wait_ge(ya_ready, NT * l + t + 1)
                    if n in (H + 3, 2 * H + 3, 3 * H + 3):
                        t = n // H - 1
                        sum_squares(l, "oc", t, TILES[t][1], H)
                    if n in (H + 4, 2 * H + 4, 3 * H + 4):
                        t = n // H - 2
                        rows = TILES[t][1]
                        v, g = head_norm("oc", t, rows, bsub)
                        V.tensor_tensor(Yc[0:rows, t].rearrange("p (g d) -> p g d", g=H), v, g, ALU.mult).then_inc(yc_ready, 1)
                        dve.wait_ge(yc_ready, NT * l + t + 1)

                def add_to_x(job):
                    for t, (t0, rows) in enumerate(TILES):
                        for full, free, R, lo in ((A_full, A_free, RA_, 0), (D_full, D_free, RD_, 512)):
                            dve.wait_ge(full, R.filled(job(t)))
                            xs = x[0:rows, t, lo:lo + 512]
                            V.tensor_tensor(xs, xs, R.bank(job(t))[0:rows, :], ALU.add).then_inc(free, 1)

                add_to_x(lambda t: ("wo", l, t))
                outputs_left(dve, l)
                if l:
                    norm(2 * l + 1)
                else:
                    norm_split(1)
                    for q in range(len(CUTS) + 3):
                        if q in (DOWN0 + HALF + 2, len(CUTS) + 2):
                            for job, o in DOWN_BANKS[q == len(CUTS) + 2]:
                                if job == "D":
                                    dve.wait_ge(D_full, RD_.filled(("dT", o)))
                                    V.tensor_copy(xT[:, o, :], RD_.bank(("dT", o))[:, 0:T]).then_inc(D_free, 1)
                        if q < len(CUTS):
                            dve.wait_ge(cut_hi_ready, q + 1)
                            V.tensor_tensor(split_cut(cut_lo, q), raw_cut(q), split_cut(cut_hi, q).bitcast(F32), ALU.subtract).then_inc(cut_lo_ready, 1)
                        if q % 2 == 0 and CR < q <= DOWN0 + CR:
                            f = (q - CR - 1) // 2
                            dve.wait_ge(D_full, RD_.filled(("u", f)))
                            dve.wait_ge(A_free, RA_.emptied(("g", f)))
                            if f:
                                dve.wait_ge(hT_ready, f)
                            V.tensor_tensor(prod[:], sg[:, f % 2], RD_.bank(("u", f))[:, 0:T], ALU.mult).then_inc(D_free, 1)
                            dve.wait_ge(D_free, RD_.emptied(("u", f)))
                            step(V.tensor_copy(hT_hi[:, f, :], prod[:]))
                            V.tensor_tensor(hT_lo[:, f, :], prod[:], hT_hi[:, f, :].bitcast(F32), ALU.subtract).then_inc(hT_ready, 1)
                    add_to_x(lambda t: ("dn", t))

            dve.nop().then_inc(lo_ready, PR)
            V.memset(rank[TILES[2][1]:P, 2], 0.0)
            step(V.memset(lgs[TILES[2][1]:P, 2], 0.0))
            for t, (t0, rows) in enumerate(TILES):
                dve.wait_ge(D_full, RD_.filled(("lg", t)))
                V.tensor_copy(lgs[0:rows, t], RD_.bank(("lg", t))[0:rows, 0:NE]).then_inc(D_free, 1)
            dve.wait_ge(D_free, RD_.emptied(("lg", 2)))
            for t in range(NT):
                last = V.max(top[:, t], lgs[:, t])
            step(last)
            for t in range(NT):
                last = V.max_index(topi[:, t], top[:, t], lgs[:, t])
            step(last)
            V.tensor_tensor(gd[:, :, 0:1], top[:, :, 1:2], top[:, :, 0:1], ALU.subtract).then_inc(gate_in, 1)
            step(V.tensor_copy(topf[:], topi[:]))
            for k in range(2):
                last = V.tensor_tensor(oh[:, :, k], C("iota8").unsqueeze(1).to_broadcast([P, NT, NE]),
                                       topf[:, :, k:k + 1].to_broadcast([P, NT, NE]), ALU.is_equal)
            step(last)
            V.tensor_tensor(M[:], oh[:, :, 0], oh[:, :, 1], ALU.add).then_inc(M_ready, 1)
            for t, (t0, rows) in enumerate(TILES):
                dve.wait_ge(D_full, RD_.filled(("rk", t)))
                V.tensor_copy(rank[0:rows, t], RD_.bank(("rk", t))[0:rows, 0:NE]).then_inc(D_free, 1)
            dve.wait_ge(D_free, RD_.emptied(("rk", 2)))
            dve.wait_ge(M_ready, 1)
            step(V.scalar_tensor_tensor(out=rankm[:], in0=rank[:], scalar=1.0, in1=M[:], op0=ALU.add, op1=ALU.mult))
            step(V.tensor_scalar(rankm[:], rankm[:], -1.0, None, ALU.add))
            dve.wait_ge(D_full, RD_.filled(("cnt",)))
            V.tensor_reduce(cntm[0:1, 0:1], RD_.bank(("cnt",))[0:1, 0:NE], AX_X, ALU.max).then_inc(D_free, 1)
            dve.wait_ge(D_free, RD_.emptied(("cnt",)))
            for b in range(1, MAXB):
                step(V.tensor_scalar(cntm[0:1, b:b + 1], cntm[0:1, 0:1], float(P * b), float(NE // 2), ALU.is_gt, ALU.mult))
            step(V.tensor_tensor(cntm[0:1, 3:4], cntm[0:1, 1:2], cntm[0:1, 2:3], ALU.add))
            step(V.tensor_copy(npair[0:1, 1:2], cntm[0:1, 3:4]))
            V.tensor_scalar(npair[0:1, 0:1], cntm[0:1, 3:4], float(NE // 2), None, ALU.add).then_inc(pairs_ready, 1)
            step(V.memset(idx[:], 0))
            for t, (t0, rows) in enumerate(TILES):
                V.memset(tokb[:, t, 0:1], float(t0))
                last = V.tensor_copy(tokb[:, t, 1:2], C("tok")[:, 0:1])
            step(last)
            for e in range(NE):
                if e >= 2:
                    dve.wait_ge(G_used, e - 1)
                for t, (t0, rows) in enumerate(TILES):
                    last = V.tensor_scalar(G[0:rows, e % 2, t], C("slot", rows), rankm[0:rows, t, e:e + 1], None, ALU.is_equal)
                last.then_inc(G_ready, 1)
                if e == 1:
                    dve.wait_ge(D_full, RD_.filled(("idx0",)))
                    V.tensor_reduce(idx0f[:], RD_.bank(("idx0",))[:, 0:2], AX_X, ALU.add).then_inc(D_free, 1)
                    dve.wait_ge(D_free, RD_.emptied(("idx0",)))
                    V.tensor_copy(idx0[:], idx0f[:]).then_inc(idx0_ready, 1)

            def piece_lo(i):
                V.tensor_tensor(split_lo[:, i % SR, :], raw[:, (i % PR) * PIECE:(i % PR + 1) * PIECE],
                                split_hi[:, i % SR, :].bitcast(F32), ALU.subtract).then_inc(lo_ready, 1)

            dve.wait_ge(hi_ready, 1)
            piece_lo(0)
            dve.wait_ge(D_full, RD_.filled(("idx",)))
            step(V.tensor_reduce(idxf[:], RD_.bank(("idx",))[:, 0:2 * MAXB * NE].rearrange("p (n c) -> p n c", c=2), AX_X, ALU.add))
            V.tensor_copy(idx[:, 0:MAXB * NE], idxf[:]).then_inc(idx_ready, 1)
            for i in range(1, SR):
                dve.wait_ge(hi_ready, i + 1)
                piece_lo(i)

            dve.nop().then_inc(u_free, 1)
            dve.wait_ge(pairs_ready, 1)
            pairs = dve.value_load(npair[0:1, 0:1], min_val=NE // 2, max_val=NE // 2 * MAXB)
            tb = [banks[4], banks[5]]

            def xg_lo(first, base):
                for k in range(KB):
                    if k % 4 == 0:
                        dve.wait_ge(th_ready, base + (first + k // 4 + 1))
                    b = tb[(first + k // 4) % 2]
                    last = V.scalar_tensor_tensor(out=xgT_lo[:, k, :], in0=b[:, 128 * (k % 4):128 * (k % 4) + 128], scalar=gcol(3)[:, k:k + 1],
                                                  in1=xgT_hi[:, k, :].bitcast(F32), op0=ALU.mult, op1=ALU.subtract)
                    if k % 4 == 3:
                        last.then_inc(t_free, 1)

            xg_lo(0, 0)
            step(V.tensor_tensor(rtmp[:], oh[:], rank[:].unsqueeze(2).to_broadcast([P, NT, 2, NE]), ALU.mult))
            step(V.tensor_reduce(rk2[:], rtmp[:], AX_X, ALU.add))
            step(V.scalar_tensor_tensor(out=posf[:], in0=topf[:, :, 0:2], scalar=float(P), in1=rk2[:], op0=ALU.mult, op1=ALU.add))
            for b in range(1, MAXB):
                step(V.tensor_scalar(ov[:], rk2[:], float(P * b), float(NE * P - P), ALU.is_ge, ALU.mult))
                step(V.tensor_tensor(posf[:], posf[:], ov[:], ALU.add))
            V.tensor_copy(pos[:], posf[:]).then_inc(pos_ready, 1)
            dve.wait_ge(gate_out, 1)
            step(V.tensor_scalar(gd[:, :, 0:1], gd[:, :, 1:2], 1.0, None, ALU.add))
            step(V.reciprocal(gd[:, :, 2:3], gd[:, :, 0:1]))
            step(V.tensor_tensor(gd[:, :, 3:4], gd[:, :, 1:2], gd[:, :, 2:3], ALU.mult))

            with dve.Fori(0, pairs) as ip:
                with dve.If(ip > 0):
                    for i in range(SR):
                        dve.wait_ge(hi_ready, ip * (2 * NP) + (i + 1))
                        piece_lo(i)
                for i in range(2 * NP):
                    h, q = divmod(i, NP)
                    if i >= SR:
                        dve.wait_ge(hi_ready, ip * (2 * NP) + (i + 1))
                        piece_lo(i)
                    if q % 4 == 2 and 1 <= q // 4 <= FC:
                        j = q // 4 - 1
                        m = FC * h + j
                        dve.wait_ge(piece_used, ip * (2 * NP) + (NP * h + 4 * j + 4 + SR))
                        dve.wait_ge(g_free, ip * (2 * FC) + (m + 2))
                        dve.wait_ge(t_full, ip * 18 + (2 + 9 * h + max(j - 1, 0)))
                        V.tensor_tensor(hm[:, m % 2, :], hs[:, m % 2, :], banks[2 + m % 2][:], ALU.mult).then_inc(u_free, 1)
                    if q in HT_AT:
                        j = HT_AT.index(q)
                        n = 2 + 9 * h + j
                        dve.wait_ge(th_ready, ip * 18 + (n + 1))
                        V.tensor_tensor(hmT_lo[:, 4 * j:4 * j + 4, :].rearrange("p b n -> p (b n)"), tb[n % 2][:],
                                        hmT_hi[:, 4 * j:4 * j + 4, :].rearrange("p b n -> p (b n)").bitcast(F32), ALU.subtract).then_inc(t_free, 1)
                    if q == X_AT:
                        xg_lo(9 * h + 9, ip * 18)

            for t, (t0, rows) in enumerate(TILES):
                for k in range(2):
                    dve.wait_ge(cmb_in[2 * t + k], 16)
                    xs = x[0:rows, t, :]
                    V.scalar_tensor_tensor(out=xs, in0=cmb[0:rows, 2 * t + k, :], scalar=gd[0:rows, t, 2 + k:3 + k], in1=xs,
                                           op0=ALU.mult, op1=ALU.add).then_inc(cmb_used, 1)
                    dve.wait_ge(cmb_used, 2 * t + k + 1)

        @block.tensor
        def _(pe):
            TE = nc.tensor
            owed = [0]
            step = Steps(pe, pe_step)

            def issue(ins):
                if owed[0]:
                    ins.then_inc(unit_used, 1)
                    owed[0] -= 1
                return ins

            def mm(out, lhsT, rhs, start, stop):
                return issue(TE.matmul(out, lhsT, rhs, start=start, stop=stop))

            def tr(out, in_, rows):
                return issue(TE.transpose(out, in_, ident[0:rows, 0:rows]))

            def unit(u):
                n = UNIT[u]
                pe.wait_ge(ring_full[n % RING], 16 * (n // RING + 1))
                return ring[:, n % RING, :]

            def done():
                assert owed[0] == 0
                owed[0] = 1

            pe.wait_ge(const_in, 16)
            pe.wait_ge(prow_in, 64)
            tr(RA_.begin(pe, ("par",))[:, 0:48], prow, 48).then_inc(A_full, 1)
            pe.wait_ge(brow_in, 16 * 8)
            for i, (R, full) in enumerate(((RA_, A_full), (RD_, D_full))):
                mm(R.begin(pe, ("bcast", i))[:, 0:480], C("ones", 1), brow[0:1, 480 * i:480 * i + 480], True, True).then_inc(full, 1)

            def norm(i):
                for t, (t0, rows) in enumerate(TILES):
                    pe.wait_ge(xhat_ready, 3 * i + t + 1)
                    for R, full, k0 in ((RA_, A_full, 0), (RD_, D_full, 4)):
                        b = R.begin(pe, ("xt", i, t))
                        for k in range(4):
                            last = tr(b[:, 128 * k:128 * k + rows], xhat[0:rows, t, 128 * (k0 + k):128 * (k0 + k) + 128], rows)
                        last.then_inc(full, 1)

            def xT_ready(i):
                pe.wait_ge(A_free, RA_.emptied(("xt", i, 2)))
                pe.wait_ge(D_free, RD_.emptied(("xt", i, 2)))

            for l in range(DEPTH):
                norm(2 * l)
                xT_ready(2 * l)
                if l == 0:
                    pe.wait_ge(wga_in, 16 * 2)

                def features(R, full, job, lhs, rows):
                    b = R.begin(pe, job)[0:rows, 0:T]
                    for k in range(KB):
                        last = mm(b, lhs(k), xT[:, k, :], k == 0, k == KB - 1)
                    last.then_inc(full, 1)

                def tokens(R, full, what):
                    w = unit((what, l))
                    for t, (t0, rows) in enumerate(TILES):
                        b = R.begin(pe, (what, l, t))[0:rows, 0:384]
                        for k in range(KB):
                            last = mm(b, xT[:, k, t0:t0 + rows], w[:, 384 * k:384 * k + 384], k == 0, k == KB - 1)
                        last.then_inc(full, 1)
                    done()

                def heads_T(job, t, src):
                    rows = TILES[t][1]
                    b = RA_.begin(pe, job)
                    for h in range(H):
                        last = tr(b[:, 128 * h:128 * h + rows], src[0:rows, 2 * h:2 * h + 2, :].rearrange("p c d -> p (c d)"), rows)
                    last.then_inc(A_full, 1)

                features(RA_, A_full, ("ga", l), lambda k: wga[:, l, k, :], GR)
                tokens(RA_, A_full, "qk")
                for t in range(NT):
                    pe.wait_ge(A_free, RA_.emptied(("qk", l, t)))
                    heads_T(("qkt", l, t), t, qkp[:, t])
                w = unit(("bc", l))
                for i, name in enumerate(("bb", "cb")):
                    for b in range(2):
                        features(RA_, A_full, (name, l, b), lambda k, o=256 * i + 128 * b, w=w: w[:, 512 * k + o:512 * k + o + 128], P)
                done()
                if l == 0:
                    pe.wait_ge(w_small, 16 * 5)
                for r in range(2):
                    pe.wait_ge(A_free, RA_.emptied(("ga", l)))
                    TE.matmul(RD_.begin(pe, ("gl", l, r))[:, 0:T], wg2[:, l, r, :], gaT, start=True, stop=True).then_inc(D_full, 1)
                w = unit(("hb", l))
                for b in range(2):
                    features(RD_, D_full, ("hb", l, b), lambda k, o=128 * b, w=w: w[:, 256 * k + o:256 * k + o + 128], P)
                done()

                tokens(RD_, D_full, "kc")
                tokens(RD_, D_full, "qc")
                pe.wait_ge(past_in, 32 * (l + 1))
                heads_T(("pk", l), 0, pkr)
                for t in range(NT):
                    pe.wait_ge(rope_ready, 6 * l + t + 1)
                    heads_T(("kt", l, t), t, krope[:, t])
                tokens(RA_, A_full, "vc")
                for t in range(NT):
                    pe.wait_ge(rope_ready, 6 * l + 3 + t + 1)
                    heads_T(("qt", l, t), t, qrope[:, t])
                tokens(RA_, A_full, "va")
                tokens(RD_, D_full, "ra")
                pe.wait_ge(gk_ready, 2 * l + 2)
                for t, (t0, rows) in enumerate(TILES):
                    b = RA_.begin(pe, ("kd", l, t))
                    for r in range(2):
                        last = tr(b[0:rows, 256 * r:256 * r + 128], ed[:, r, t0:t0 + rows], P)
                    last.then_inc(A_full, 1)
                for t, (t0, rows) in enumerate(TILES):
                    b = RD_.begin(pe, ("att", l, t))
                    for q0 in (0, HW):
                        for c in range(rows // CH):
                            a, p0 = t0 + CH * c, CH * c
                            for r in range(2):
                                o = CH * (2 * r + q0 // HW)
                                last = mm(b[p0:p0 + CH, o:o + CH], ek[q0:q0 + DK, r, a:a + CH], eq[q0:q0 + DK, r, a:a + CH], True, True)
                        if q0 == 0:
                            step(last)
                    last.then_inc(D_full, 1)
                pe.wait_ge(A_free, RA_.emptied(("kd", l, 2)))
                for c, (t, p0) in enumerate(CHUNKS):
                    b = RD_.begin(pe, ("U", l, c))
                    for h in range(H):
                        r, q0 = h // 2, HW * (h % 2)
                        last = mm(b[q0:q0 + HW, DV * r:DV * r + DV], kdn[p0:p0 + CH, t, r, q0:q0 + HW], va[p0:p0 + CH, t, DV * h:DV * h + DV], True, True)
                    last.then_inc(D_full, 1)
                for t, (t0, rows) in enumerate(TILES):
                    b = RD_.begin(pe, ("oa", l, t))
                    if t == 0:
                        pe.wait_ge(D_free, RD_.emptied(("att", l, 2)))
                    pe.wait_ge(D_free, RD_.emptied(("U", l, {0: 0, 1: 2, 2: 4}[t])))
                    work = {0: [], HW: []}
                    late = []
                    for c in range(rows // CH):
                        p0, a = CH * c, t0 + CH * c
                        before = 5 if t == 2 else 2 * t + c - 1
                        inner = [(b[p0:p0 + CH, DV * h:DV * h + DV], att[p0:p0 + CH, t, h, :], va[p0:p0 + CH, t, DV * h:DV * h + DV]) for h in range(H)]
                        work[p0] += [(m, i == 0, c) for i, m in enumerate(inner)]
                        if before >= 0:
                            for h in range(H):
                                r, q0 = h // 2, HW * (h % 2)
                                m = (b[p0:p0 + CH, DV * h:DV * h + DV], qb[q0:q0 + DK, r, a:a + CH], S[q0:q0 + DK, before, r, :])
                                (late if q0 < p0 else work[q0]).append((m, False, c))
                    groups = [g for g in (work[0], work[HW], late) if g]
                    for i, g in enumerate(groups):
                        for k, ((o, lhsT, rhs), first, c) in enumerate(g):
                            left = [x[2] for x in g[k + 1:]] + [x[2] for later in groups[i + 1:] for x in later]
                            last = mm(o, lhsT, rhs, first, c not in left)
                        if i < len(groups) - 1:
                            step(last)
                    last.then_inc(D_full, 1)

                for n in range(NT * H + 3):
                    if n < NT * H:
                        t, h = divmod(n, H)
                        t0, rows = TILES[t]
                        if n == 0:
                            pe.wait_ge(A_free, RA_.emptied(("qt", l, 2)))
                        b = RS_.begin(pe, ("s", l, n)).rearrange("p (c k) -> p c k", c=2)
                        for c in range(2):
                            if c:
                                step(last)
                            q0 = HW * c
                            q = qT[q0:q0 + DK, h, t0:t0 + rows]
                            if t < 2:
                                keys = P * (t + 1)
                                mm(b[:, c, 0:keys], q, kT[q0:q0 + DK, h, 0:keys], True, False)
                                last = mm(b[:, c, keys - CH:keys], C("rowsel")[q0:q0 + 1], C("neg")[q0:q0 + 1], False, True)
                            else:
                                mm(b[0:rows, c, 0:PAST], q, pkT[q0:q0 + DK, h, :], True, True)
                                last = mm(b[0:rows, c, PAST:PAST + DEC], q, kT[q0:q0 + DK, h, SEQ:T], True, True)
                        last.then_inc(S_full, 1)
                    if 2 <= n <= NT * H + 1:
                        m = n - 2
                        t = m // H
                        rows = TILES[t][1]
                        pe.wait_ge(am_ready, NT * H * l + m + 1)
                        b = RA_.begin(pe, ("at", l, m))
                        for i, nk in enumerate([[128], [128, 128], [128, 64]][t]):
                            last = tr(b[0:nk, 128 * i:128 * i + rows], am[0:rows, m % 2, 128 * i:128 * i + nk], rows)
                        last.then_inc(A_full, 1)
                    if n >= 3:
                        m = n - 3
                        t, h = divmod(m, H)
                        rows = TILES[t][1]
                        pe.wait_ge(A_free, RA_.emptied(("at", l, m)))
                        b = RD_.begin(pe, ("oc", l, t)) if h == 0 else RD_.bank(("oc", l, t))
                        vs = [[(vc, 0)], [(vc, 0), (vc, 1)], [(pv, l), (vc, 2)]][t]
                        for i, (v, at) in enumerate(vs):
                            nk = DEC if t == 2 and i == 1 else P
                            last = mm(b[0:rows, DV * h:DV * h + DV], aT[0:nk, m % 2, i, 0:rows], v[0:nk, at, DV * h:DV * h + DV], i == 0, i == len(vs) - 1)
                        if h == H - 1:
                            last.then_inc(D_full, 1)

                for what, src, ready in (("ya", Ya, ya_ready), ("yc", Yc, yc_ready)):
                    for t, (t0, rows) in enumerate(TILES):
                        pe.wait_ge(ready, NT * l + t + 1)
                        b = RA_.begin(pe, (what, l, t))
                        for k in range(3):
                            last = tr(b[:, 128 * k:128 * k + rows], src[0:rows, t, 128 * k:128 * k + 128], rows)
                        last.then_inc(A_full, 1)

                def down(job, blocks, lhs, unit_of):
                    bs = {}
                    for t in range(NT):
                        bs[t, 0] = RA_.begin(pe, job(t))
                        bs[t, 1] = RD_.begin(pe, job(t))
                    for b in range(blocks):
                        if b % 4 == 0:
                            w = unit(unit_of(b // 4))
                        for t, (t0, rows) in enumerate(TILES):
                            for i, full in enumerate((A_full, D_full)):
                                o = 1024 * (b % 4) + 512 * i
                                last = mm(bs[t, i][0:rows, :], lhs(b, t0, rows), w[:, o:o + 512], b == 0, b == blocks - 1)
                                if b == blocks - 1:
                                    last.then_inc(full, 1)
                        if b % 4 == 3 or b == blocks - 1:
                            done()

                pe.wait_ge(A_free, RA_.emptied(("yc", l, 2)))
                pe.wait_ge(conv_ready, l + 1)
                down(lambda t: ("wo", l, t), KB,
                     lambda b, t0, rows: (yb[:, b - 3, t0:t0 + rows] if b in (3, 4) else yT[:, b, t0:t0 + rows]),
                     lambda j: ("wo", l, j))

                norm(2 * l + 1)
                xT_ready(2 * l + 1)
                if l == 0:
                    def three(q, out, k, a, hi, lo, start, stop):
                        w_hi, w_lo = split_cut(cut_hi, q)[:, k, a:a + P], split_cut(cut_lo, q)[:, k, a:a + P]
                        mm(out, w_hi, hi, start, False)
                        mm(out, w_lo, hi, False, False)
                        return mm(out, w_hi, lo, False, stop)

                    for q, (u, kind, which) in enumerate(CUTS[:DOWN0]):
                        pe.wait_ge(cut_lo_ready, q + 1)
                        R, full = (RA_, A_full) if kind == "g" else (RD_, D_full)
                        b = R.begin(pe, (kind, which))[:, 0:T]
                        for k in range(KB):
                            last = three(q, b, k, 0, xT_hi[:, k, :], xT_lo[:, k, :], k == 0, k == KB - 1)
                        last.then_inc(full, 1)
                    for q, (u, kind, (c, m)) in enumerate(CUTS[DOWN0:], DOWN0):
                        pe.wait_ge(cut_lo_ready, q + 1)
                        for i in range(2):
                            if c == 0:
                                pe.wait_ge(hT_ready, 2 * m + i + 1)
                            for ring_name, o in DOWN_BANKS[c]:
                                R, full = (RA_, A_full) if ring_name == "A" else (RD_, D_full)
                                b = R.begin(pe, ("dT", o)) if m + i == 0 else R.bank(("dT", o))
                                end = m == HALF - 1 and i == 1
                                last = three(q, b[:, 0:T], i, P * (o % 4), hT_hi[:, 2 * m + i, :], hT_lo[:, 2 * m + i, :], m + i == 0, end)
                                if end:
                                    last.then_inc(full, 1)
                        if m < HALF - 1:
                            last.then_inc(cut_used, 1)
                    pe.wait_ge(A_free, RA_.emptied(("dT", 5)))
                    pe.wait_ge(D_free, RD_.emptied(("dT", 7)))
                    for t, (t0, rows) in enumerate(TILES):
                        for R, full, o0 in ((RA_, A_full, 0), (RD_, D_full, 4)):
                            b = R.begin(pe, ("dn", t))
                            for o in range(4):
                                last = tr(b[0:rows, P * o:P * o + P], xT[:, o0 + o, t0:t0 + rows], P)
                            last.then_inc(full, 1)

            for t, (t0, rows) in enumerate(TILES):
                b = RD_.begin(pe, ("lg", t))
                for k in range(KB):
                    last = mm(b[0:rows, 0:NE], xT[:, k, t0:t0 + rows], wr[:, k, :], k == 0, k == KB - 1)
                last.then_inc(D_full, 1)
            for t, (t0, rows) in enumerate(TILES):
                pe.wait_ge(M_ready, 1)
                b = RD_.begin(pe, ("rk", t))[0:rows, 0:NE]
                for s in range(t):
                    mm(b, C("ones")[:, 0:rows], M[:, s, :], s == 0, False)
                mm(b, C("tri", rows)[:, 0:rows], M[0:rows, t, :], t == 0, True).then_inc(D_full, 1)
            b = RD_.begin(pe, ("cnt",))[:, 0:NE]
            for t, (t0, rows) in enumerate(TILES):
                last = mm(b, C("ones", rows), M[0:rows, t, :], t == 0, t == NT - 1)
            last.then_inc(D_full, 1)
            tb = [banks[4], banks[5]]
            assert RD_.bank(("idx",)) is banks[3]

            def xg_T(first, base):
                for i in range(2):
                    if base is not None:
                        pe.wait_ge(t_free, base + (first + i - 1))
                    for k in range(4):
                        last = tr(tb[(first + i) % 2][:, 128 * k:128 * k + 128], xg[:, 512 * i + 128 * k:512 * i + 128 * k + 128], P)
                    last.then_inc(t_full, 1)

            pe.wait_ge(G_ready, 1)
            b = RD_.begin(pe, ("idx0",))
            for t, (t0, rows) in enumerate(TILES):
                last = mm(b[:, 0:2], G[0:rows, 0, t, 0:P], tokb[0:rows, t, :], t == 0, t == NT - 1)
            last.then_inc(D_full, 1)
            b = RD_.begin(pe, ("idx",))
            for e in range(NE):
                pe.wait_ge(G_ready, e + 1)
                for s in range(MAXB):
                    for t, (t0, rows) in enumerate(TILES):
                        o = 2 * (NE * s + e)
                        last = mm(b[:, o:o + 2], G[0:rows, e % 2, t, P * s:P * s + P], tokb[0:rows, t, :], t == 0, t == NT - 1)
                if e < NE - 1:
                    last.then_inc(G_used, 1)
            last.then_inc(D_full, 1)
            pe.wait_ge(D_free, RD_.emptied(("idx0",)))
            pe.wait_ge(xg_in, 16)
            xg_T(0, None)
            assert owed[0] == 0

            pe.wait_ge(A_free, RA_.count)
            pe.wait_ge(D_free, RD_.count - 1)
            pe.wait_ge(idx_ready, 1)
            pe.wait_ge(pairs_ready, 1)
            pairs = pe.value_load(npair[0:1, 0:1], min_val=NE // 2, max_val=NE // 2 * MAXB)
            pe.nop().then_inc(piece_used, SR)

            with pe.Fori(0, pairs) as ip:
                for i in range(2 * NP):
                    h, q = divmod(i, NP)
                    hi, lo = split_hi[:, i % SR, :], split_lo[:, i % SR, :]
                    j, half = q // 2, q % 2
                    if q == 0:
                        pe.wait_ge(t_free, ip * 18 + (2 + 9 * h))
                    if j < 2 * FC and half == 0:
                        m = FC * h + j // 2
                        pe.wait_ge(u_free if j % 2 else g_free, ip * (2 * FC) + max(m, 1))
                    if q == 4 * FC:
                        pe.wait_ge(y_free, ip * 2 + (h + 1))
                    if q >= 4 * FC and half == 0:
                        pe.wait_ge(t_free, ip * 18 + (2 + 9 * h + j - 2 * FC + 1))
                    pe.wait_ge(lo_ready, ip * (2 * NP) + (i + 1 + PR))
                    if j < 2 * FC:
                        o = banks[2 * (j % 2) + (FC * h + j // 2) % 2][:]
                        for k in range(4):
                            kk = 4 * half + k
                            c = slice(512 * k, 512 * k + 512)
                            TE.matmul(o, xgT_hi[:, kk, :], hi[:, c], start=kk == 0, stop=False)
                            TE.matmul(o, xgT_hi[:, kk, :], lo[:, c], start=False, stop=False)
                            last = TE.matmul(o, xgT_lo[:, kk, :], hi[:, c], start=False, stop=kk == KB - 1)
                    else:
                        for k in range(2):
                            b = 4 * (j - 2 * FC) + 2 * half + k
                            cs = [slice(1024 * k + 512 * n, 1024 * k + 512 * n + 512) for n in range(2)]
                            for n in range(2):
                                TE.matmul(banks[6 + n][:], hmT_hi[:, b, :], hi[:, cs[n]], start=b == 0, stop=False)
                                TE.matmul(banks[6 + n][:], hmT_hi[:, b, :], lo[:, cs[n]], start=False, stop=False)
                            for n in range(2):
                                last = TE.matmul(banks[6 + n][:], hmT_lo[:, b, :], hi[:, cs[n]], start=False, stop=b == FEB - 1)
                    last.then_inc(piece_used, 1)
                    if q in [a - 4 for a in HT_AT]:
                        c = HT_AT.index(q + 4)
                        m, n = FC * h + c, 2 + 9 * h + c
                        pe.wait_ge(u_free, ip * (2 * FC) + (m + 2))
                        pe.wait_ge(t_free, ip * 18 + (n - 1))
                        for k in range(4):
                            last = TE.transpose(tb[n % 2][:, 128 * k:128 * k + 128], hm[:, m % 2, 128 * k:128 * k + 128], ident)
                        last.then_inc(t_full, 1)
                    if q == X_AT - 4:
                        pe.wait_ge(xg_in, ip * 32 + 16 * (h + 2))
                        xg_T(9 * h + 9, ip * 18)


_INS = ['x_prompt', 'x_sample', 'state_gla', 'state_conv', 'cache_k', 'cache_v', 'g_mix', 'w_in', 'w_g2', 'b_g2', 'g_gla',
        'w_conv', 'g_q', 'g_k', 'lambda_q1', 'lambda_k1', 'lambda_q2', 'lambda_k2', 'g_sub', 'w_out', 'g_ffn',
        'ffn_w_gate', 'ffn_w_up', 'ffn_w_down', 'w_router', 'moe_w_gate', 'moe_w_up', 'moe_w_down']
_OUTS = [(1, SEQ, D), (1, DEC, D), (DEPTH, 1, SEQ, H, 2, DK), (DEPTH, 1, SEQ, H, DV), (DEPTH, 1, H, DK, DV), (DEPTH, 1, 2, 256),
         (DEPTH, 1, DEC, H, 2, DK), (DEPTH, 1, DEC, H, DV), (DEPTH, 1, H, DK, DV), (DEPTH, 1, 2, 256)]


def _constants():
    c = np.zeros((P, CONST_W), np.float32)

    def at(name):
        a, w = CONST[name]
        return c[:, a:a + w]

    p = np.arange(P)
    at("ident")[:] = np.eye(P)
    at("tri")[:] = p[:, None] < p[None, :]
    at("ones")[:] = 1
    at("scan")[:] = np.arange(T) % CH != 0
    half = DK // 2
    freq = np.float32(10000.0) ** (-np.arange(half, dtype=np.float32) / np.float32(half))
    for t, (t0, rows) in enumerate(TILES):
        position = (t0 + p if t < 2 else PAST + p).astype(np.float32)
        angle = position[:, None] * freq[None, :]
        cos, sin = np.cos(angle), np.sin(angle)
        at("cc")[:, t * DK:(t + 1) * DK] = np.concatenate([cos, cos], 1)
        at("ss")[:, t * DK:(t + 1) * DK] = np.concatenate([-sin, sin], 1)
        at("tok")[:, t] = t0 + p
    at("iota8")[:] = np.arange(8)
    at("slot")[:] = np.arange(MAXB * P)
    at("attm")[:] = np.tile((p % CH)[:, None] <= np.arange(CH)[None, :], (1, H))
    at("rowsel")[:] = p < CH
    at("neg")[:] = -1e30
    return c


def kernel(**inputs):
    import concourse.bacc as _bacc
    from concourse.bass_utils import run_bass_kernel_spmd as _run

    nc = _bacc.Bacc("TRN2", target_bir_lowering=False, num_devices=1)
    arrays = {name: np.ascontiguousarray(inputs[name]) for name in _INS}
    arrays["const"] = _constants()
    aps = {name: nc.dram_tensor(name, a.shape, mybir.dt.from_np(a.dtype), kind="ExternalInput").ap() for name, a in arrays.items()}
    outs = [nc.dram_tensor(f"out_{i}", shape, F32, kind="ExternalOutput").ap() for i, shape in enumerate(_OUTS)]
    build(nc, aps, outs)
    r = _run(nc, [arrays], core_ids=[0])
    return tuple(r.results[0][f"out_{i}"] for i in range(len(_OUTS)))
```
